# Optimizing a Trainium2 kernel written in Bass

```python
import math
import jax
import jax.numpy as jnp
from jax import lax
import numpy as np

D_MODEL = 1024
BATCH = 1
SEQ = 2048
DEPTH = 1

D_MIX = D_MODEL
D_CONV = D_MIX // 2
D_ATTN = D_MIX - D_CONV
HEAD_DIM = 64
N_HEADS = D_ATTN // HEAD_DIM
CONV_K = 3
IN_COLS = 3 * D_CONV + 3 * D_ATTN
QBLK = 128
N_EXPERTS = 32
N_GROUPS = 8
EXPERTS_PER_GROUP = N_EXPERTS // N_GROUPS
TOP_K = 2
D_EXPERT = 512
MOE_BLK = 128
DEEPNORM_ALPHA = (2.0 * DEPTH) ** 0.25
DEEPNORM_BETA = (8.0 * DEPTH) ** -0.25
LN_EPS = 1e-5
RMS_EPS = 1e-6

kernel_name = "hybrid_conv_stickbreaking_sharedrouter_moe_deepnorm"

def layer_norm(x, g, b):
    xf = x.astype(jnp.float32)
    mu = jnp.mean(xf, axis=-1, keepdims=True)
    var = jnp.mean(jnp.square(xf - mu), axis=-1, keepdims=True)
    y = (xf - mu) * lax.rsqrt(var + LN_EPS) * g.astype(jnp.float32) + b.astype(jnp.float32)
    return y.astype(x.dtype)

def rms_norm(x, g):
    xf = x.astype(jnp.float32)
    y = xf * lax.rsqrt(jnp.mean(jnp.square(xf), axis=-1, keepdims=True) + RMS_EPS)
    return (y * g.astype(jnp.float32)).astype(x.dtype)

def causal_short_conv(u, w):
    c = u.shape[-1]
    return lax.conv_general_dilated(
        u, w[:, None, :].astype(u.dtype), window_strides=(1,),
        padding=((CONV_K - 1, 0),), dimension_numbers=("NWC", "WIO", "NWC"),
        feature_group_count=c)

def stick_breaking_attention(q, k, v):
    bsz, s, _ = q.shape
    nb = s // QBLK
    scale = 1.0 / math.sqrt(HEAD_DIM)
    qh = q.reshape(bsz, s, N_HEADS, HEAD_DIM).transpose(0, 2, 1, 3)
    kf = k.reshape(bsz, s, N_HEADS, HEAD_DIM).transpose(0, 2, 1, 3).astype(jnp.float32)
    vf = v.reshape(bsz, s, N_HEADS, HEAD_DIM).transpose(0, 2, 1, 3).astype(jnp.float32)
    qb = qh.reshape(bsz, N_HEADS, nb, QBLK, HEAD_DIM).transpose(2, 0, 1, 3, 4)
    kpos = jnp.arange(s)

    def block(args):
        qblk, i = args
        z = jnp.einsum("bhqd,bhkd->bhqk", qblk.astype(jnp.float32), kf) * scale
        qpos = i * QBLK + jnp.arange(QBLK)
        mask = kpos[None, :] < qpos[:, None]
        log_keep = jnp.where(mask, jax.nn.log_sigmoid(-z), 0.0)
        suffix = lax.cumsum(log_keep, axis=3, reverse=True) - log_keep
        a = jnp.where(mask, jnp.exp(jax.nn.log_sigmoid(z) + suffix), 0.0)
        return jnp.einsum("bhqk,bhkd->bhqd", a, vf)

    o = lax.map(block, (qb, jnp.arange(nb)))
    o = o.transpose(1, 0, 3, 2, 4).reshape(bsz, s, D_ATTN)
    return o.astype(q.dtype)

def route(h, router_w, router_b):
    t = h.shape[0]
    scores = jax.nn.sigmoid(jnp.matmul(h, router_w).astype(jnp.float32))
    sel = (scores + router_b.astype(jnp.float32)).reshape(t, N_GROUPS, EXPERTS_PER_GROUP)
    group_score = lax.top_k(sel, 2)[0].sum(-1)
    g = jnp.argmax(group_score, axis=-1)
    in_group = jnp.take_along_axis(sel, g[:, None, None], axis=1)[:, 0]
    _, local = lax.top_k(in_group, TOP_K)
    eidx = g[:, None] * EXPERTS_PER_GROUP + local
    w = jnp.take_along_axis(scores, eidx, axis=1)
    w = w / jnp.sum(w, axis=-1, keepdims=True)
    return eidx, w

def moe(h, router_w, router_b, w_gate, w_up, w_down):
    t, d = h.shape
    eidx, w = route(h, router_w, router_b)
    n = t * TOP_K
    flat_e = eidx.reshape(n)
    flat_t = jnp.repeat(jnp.arange(t, dtype=jnp.int32), TOP_K, total_repeat_length=n)
    flat_w = w.reshape(n)
    order = jnp.argsort(flat_e)
    se, st, sw = flat_e[order], flat_t[order], flat_w[order]
    counts = jnp.zeros((N_EXPERTS,), jnp.int32).at[flat_e].add(1)
    starts = jnp.cumsum(counts) - counts
    padded = (counts + MOE_BLK - 1) // MOE_BLK * MOE_BLK
    pends = jnp.cumsum(padded)
    pstarts = pends - padded
    dest = pstarts[se] + jnp.arange(n, dtype=jnp.int32) - starts[se]
    rows = (n + N_EXPERTS * (MOE_BLK - 1) + MOE_BLK - 1) // MOE_BLK * MOE_BLK
    nblk = rows // MOE_BLK
    buf_t = jnp.full((rows,), t, jnp.int32).at[dest].set(st)
    buf_w = jnp.zeros((rows,), jnp.float32).at[dest].set(sw)
    blk_e = jnp.clip(jnp.searchsorted(pends, jnp.arange(nblk) * MOE_BLK, side="right"),
                     0, N_EXPERTS - 1)
    hp = jnp.concatenate([h, jnp.zeros((1, d), h.dtype)], axis=0)
    xb = hp[buf_t].reshape(nblk, MOE_BLK, d)

    def expert_block(args):
        xblk, e = args
        a = jnp.matmul(xblk, w_gate[e])
        u = jnp.matmul(xblk, w_up[e])
        return jnp.matmul(jax.nn.silu(a) * u, w_down[e])

    yb = lax.map(expert_block, (xb, blk_e)).reshape(rows, d)
    out = jnp.zeros((t + 1, d), h.dtype).at[buf_t].add(yb * buf_w[:, None].astype(h.dtype))
    return out[:t]

def setup_inputs(seed: int = 0) -> dict:
    key = jax.random.key(seed)
    ks = jax.random.split(key, 18)
    nrm = jax.random.normal
    f32 = jnp.float32
    return {
        "x": nrm(ks[0], (BATCH, SEQ, D_MODEL), f32),
        "ln0_g": 1.0 + 0.02 * nrm(ks[1], (D_MODEL,), f32),
        "ln0_b": 0.02 * nrm(ks[2], (D_MODEL,), f32),
        "w_in": nrm(ks[3], (DEPTH, D_MODEL, IN_COLS), f32) * D_MODEL ** -0.5,
        "conv_w": nrm(ks[4], (DEPTH, CONV_K, D_CONV), f32) * CONV_K ** -0.5,
        "g_conv": 1.0 + 0.02 * nrm(ks[5], (DEPTH, D_CONV), f32),
        "g_attn": 1.0 + 0.02 * nrm(ks[6], (DEPTH, D_ATTN), f32),
        "w_out": nrm(ks[7], (DEPTH, D_MIX, D_MODEL), f32) * (D_MIX ** -0.5 * DEEPNORM_BETA),
        "ln_mix_g": 1.0 + 0.02 * nrm(ks[8], (DEPTH, D_MODEL), f32),
        "ln_mix_b": 0.02 * nrm(ks[9], (DEPTH, D_MODEL), f32),
        "router_w": nrm(ks[10], (D_MODEL, N_EXPERTS), f32) * D_MODEL ** -0.5,
        "router_b": 0.01 * nrm(ks[11], (N_EXPERTS,), f32),
        "w_gate": nrm(ks[12], (DEPTH, N_EXPERTS, D_MODEL, D_EXPERT), f32) * D_MODEL ** -0.5,
        "w_up": nrm(ks[13], (DEPTH, N_EXPERTS, D_MODEL, D_EXPERT), f32) * D_MODEL ** -0.5,
        "w_down": nrm(ks[14], (DEPTH, N_EXPERTS, D_EXPERT, D_MODEL), f32) * (D_EXPERT ** -0.5 * DEEPNORM_BETA),
        "ln_ffn_g": 1.0 + 0.02 * nrm(ks[15], (DEPTH, D_MODEL), f32),
        "ln_ffn_b": 0.02 * nrm(ks[16], (DEPTH, D_MODEL), f32),
    }

def reference(x, ln0_g, ln0_b, w_in, conv_w, g_conv, g_attn, w_out, ln_mix_g, ln_mix_b,
              router_w, router_b, w_gate, w_up, w_down, ln_ffn_g, ln_ffn_b):
    bsz, s, d = x.shape
    h = layer_norm(x, ln0_g, ln0_b)
    for l in range(DEPTH):
        proj = jnp.matmul(h, w_in[l])
        cb, cc, cx, q, k, v = jnp.split(
            proj, [D_CONV, 2 * D_CONV, 3 * D_CONV, 3 * D_CONV + D_ATTN,
                   3 * D_CONV + 2 * D_ATTN], axis=-1)
        conv_out = cb * causal_short_conv(cc * cx, conv_w[l])
        attn_out = stick_breaking_attention(q, k, v)
        mixed = jnp.concatenate([rms_norm(conv_out, g_conv[l]),
                                 rms_norm(attn_out, g_attn[l])], axis=-1)
        mix = jnp.matmul(mixed, w_out[l])
        h = layer_norm(DEEPNORM_ALPHA * h + mix, ln_mix_g[l], ln_mix_b[l])
        ffn = moe(h.reshape(bsz * s, d), router_w, router_b,
                  w_gate[l], w_up[l], w_down[l]).reshape(bsz, s, d)
        h = layer_norm(DEEPNORM_ALPHA * h + ffn, ln_ffn_g[l], ln_ffn_b[l])
    return h


_drawn_inputs = setup_inputs


def setup_inputs(seed=0):
    import zlib

    import numpy as np

    out = dict(_drawn_inputs(seed))
    spreads = {}
    factors = {}
    for name, (base, spread) in spreads.items():
        noise = np.random.default_rng([zlib.crc32(name.encode()), seed]).standard_normal(out[name].shape)
        drawn = base * np.exp(spread * noise) if base else spread * noise
        out[name] = jnp.asarray(drawn.astype(out[name].dtype))
    for name, factor in factors.items():
        out[name] = (out[name] * factor).astype(out[name].dtype)
    return out
```

```python
from contextlib import ExitStack

import concourse.bass as bass
from concourse import mybir

F32 = mybir.dt.float32
F32R = mybir.dt.float32r
I32 = mybir.dt.int32
U32 = mybir.dt.uint32
ALU = mybir.AluOpType
ACT = mybir.ActivationFunctionType
AX = mybir.AxisListType

P = 128
BANK = 512
SEQ, D = 2048, 1024
TILES = SEQ // P
KC = D // P
D_CONV = D // 2
D_ATTN = D - D_CONV
HEAD_DIM = 64
HEADS = D_ATTN // HEAD_DIM
CONV_K = 3
CC = D_CONV // P
TG = SEQ // BANK
EXPERTS, GROUPS, PER_GROUP, TOP_K = 32, 8, 4, 2
D_EXPERT = 512
FC = D_EXPERT // P
SLOT_BLOCKS = (SEQ * TOP_K + EXPERTS * P) // P
SLOTS = SLOT_BLOCKS * P
ALPHA = 2.0 ** 0.25
LN_EPS, RMS_EPS = 1e-5, 1e-6
SCALE = HEAD_DIM ** -0.5
EXP_CAP = 2.0 ** 60


class Memory:

    def __init__(self, nc, ctx):
        self.nc, self.ctx = nc, ctx

    def sb(self, name, shape, dt=F32):
        return self.ctx.enter_context(self.nc.sbuf_tensor(name, shape, dt))

    def ps(self, name, shape, dt=F32):
        return self.ctx.enter_context(self.nc.psum_tensor(name, shape, dt))

    def sem(self, name):
        return self.ctx.enter_context(self.nc.semaphore(name))


def skewed(engine, *stages):
    deepest = max(lag for lag, _ in stages)
    deepest += deepest % 2

    def plain(slot):
        for lag, step in stages:
            if 0 <= slot - lag < TILES:
                step(slot - lag, (slot - lag) % 2, (slot - lag) // 2)

    for slot in range(deepest):
        plain(slot)
    with engine.Fori(0, (TILES - deepest) // 2) as i:
        for parity in range(2):
            for lag, step in stages:
                ahead = deepest + parity - lag
                step(2 * i + ahead, ahead % 2, i + ahead // 2)
    for slot in range(TILES, TILES + deepest):
        plain(slot)


def load_row(engine, tile, vector, sem):
    engine.dma_start(tile, vector.partition_broadcast(P)).then_inc(sem, 16)


def norm_input(nc, const, h_tr, x, ln_g, ln_b, h_dram):
    ident = const["ident"]
    h_tr_hi, h_tr_lo = h_tr
    with ExitStack() as ctx:
        m = Memory(nc, ctx)
        rows = m.sb("n_rows", [P, TILES, D])
        gain, shift = m.sb("n_gain", [P, D]), m.sb("n_shift", [P, D])
        stats = m.sb("n_stats", [P, 2, 6])
        moments = m.sb("n_moments", [P, TILES, 2])
        rstd = m.sb("n_rstd", [P, TILES])
        offset = m.sb("n_offset", [P, TILES])
        eps = m.sb("n_eps", [P, 1])
        tr_ps = [m.ps(f"n_tr_ps{i}", [P, KC, P]) for i in range(2)]
        x_in = [m.sem(f"n_x_in{i}") for i in range(4)]
        params_in = m.sem("n_params_in")
        half_stats = m.sem("n_half_stats")
        moments_ready = m.sem("n_moments_ready")
        eps_ready = m.sem("n_eps_ready")
        std_ready = m.sem("n_std_ready")
        rstd_ready = m.sem("n_rstd_ready")
        offset_ready = m.sem("n_offset_ready")
        scaled = m.sem("n_scaled")
        gained = m.sem("n_gained")
        h_ready = m.sem("n_h_ready")
        transposed = m.sem("n_transposed")
        hi_ready = m.sem("n_hi_ready")
        tr_free = m.sem("n_tr_free")
        h_stored = m.sem("n_h_stored")
        id_zero = m.sem("n_id_zero")
        id_ready = m.sem("n_id_ready")
        group = TILES // 4
        with nc.Block() as block:

            @block.sync
            def _(sp):
                for q in range(4):
                    sp.dma_start(rows[:, q * group:(q + 1) * group, :],
                                 x[q * group * P:(q + 1) * group * P, :].rearrange("(t p) d -> p t d", p=P)
                                 ).then_inc(x_in[q], 16)
                load_row(sp, gain[:], ln_g, params_in)
                load_row(sp, shift[:], ln_b, params_in)
                with sp.Fori(0, TILES) as t:
                    sp.wait_ge(h_ready, t + 1)
                    sp.dma_start(h_dram[bass.ts(t, P), :], rows[:, t, :]).then_inc(h_stored, 16)
                sp.wait_ge(h_stored, 16 * TILES)

            @block.gpsimd
            def _(pool):
                pool.memset(ident[:], 0.0).then_inc(id_zero, 1)
                pool.wait_ge(id_zero, 1)
                pool.affine_select(out=ident[:], in_=ident[:], compare_op=ALU.not_equal, fill=1.0, base=0,
                                   pattern=[[-1, P]], channel_multiplier=1).then_inc(id_ready, 1)
                pool.wait_ge(params_in, 32)
                with pool.Fori(0, TILES) as t:
                    pool.wait_ge(gained, t + 1)
                    pool.tensor_tensor(rows[:, t, :], rows[:, t, :], shift[:], ALU.add).then_inc(h_ready, 1)

            @block.vector
            def _(dve):
                dve.memset(eps[:], LN_EPS).then_inc(eps_ready, 1)
                for q in range(4):
                    dve.wait_ge(x_in[q], 16)
                    for t in range(q * group, (q + 1) * group):
                        if t:
                            dve.wait_ge(moments_ready, t)
                        for half in range(2):
                            dve.bn_stats(stats[:, half, :], rows[:, t, half * BANK:(half + 1) * BANK]
                                         ).then_inc(half_stats, 1)
                        dve.wait_ge(half_stats, 2 * t + 2)
                        dve.bn_aggr(moments[:, t, :], stats[:]).then_inc(moments_ready, 1)
                dve.wait_ge(std_ready, 1)
                dve.reciprocal(rstd[:], rstd[:]).then_inc(rstd_ready, 1)
                dve.wait_ge(rstd_ready, 1)
                dve.scalar_tensor_tensor(offset[:], moments[:, :, 0], -1.0, rstd[:], ALU.mult, ALU.mult
                                         ).then_inc(offset_ready, 1)
                dve.wait_ge(params_in, 32)

                def gain_rows(t):
                    dve.wait_ge(scaled, t + 1)
                    dve.tensor_tensor(rows[:, t, :], rows[:, t, :], gain[:], ALU.mult).then_inc(gained, 1)

                def low_part(t, parity):
                    dve.wait_ge(hi_ready, t + 1)
                    dve.tensor_tensor(h_tr_lo[:, :, bass.ts(t, P)], tr_ps[parity][:],
                                      h_tr_hi[:, :, bass.ts(t, P)].bitcast(F32), ALU.subtract).then_inc(tr_free, 1)

                gain_rows(0)
                with dve.Fori(0, TILES // 2 - 1) as i:
                    for parity in range(2):
                        gain_rows(2 * i + parity + 1)
                        low_part(2 * i + parity, parity)
                gain_rows(TILES - 1)
                low_part(TILES - 2, 0)
                low_part(TILES - 1, 1)

            @block.scalar
            def _(act):
                act.wait_ge(moments_ready, TILES)
                act.wait_ge(eps_ready, 1)
                act.activation(rstd[:], moments[:, :, 1], ACT.Sqrt, bias=eps[:]).then_inc(std_ready, 1)
                act.wait_ge(offset_ready, 1)

                def normalise(t):
                    act.activation(rows[:, t, :], rows[:, t, :], ACT.Identity, scale=rstd[:, bass.ds(t, 1)],
                                   bias=offset[:, bass.ds(t, 1)]).then_inc(scaled, 1)

                def high_part(t, parity):
                    act.wait_ge(transposed, t + 1)
                    act.copy(h_tr_hi[:, :, bass.ts(t, P)], tr_ps[parity][:]).then_inc(hi_ready, 1)

                normalise(0)
                normalise(1)
                with act.Fori(0, TILES // 2 - 1) as i:
                    for parity in range(2):
                        normalise(2 * i + parity + 2)
                        high_part(2 * i + parity, parity)
                high_part(TILES - 2, 0)
                high_part(TILES - 1, 1)

            @block.tensor
            def _(pe):
                pe.sem_inc(tr_free, 2)
                pe.wait_ge(id_ready, 1)
                for t in range(TILES):
                    pe.wait_ge(h_ready, t + 1)
                    pe.wait_ge(tr_free, t + 1)
                    for k in range(KC):
                        last = pe.transpose(tr_ps[t % 2][:, k, :], rows[:, t, k * P:(k + 1) * P], ident[:])
                    last.then_inc(transposed, 1)


def project(nc, const, h_tr, w_in, conv_w, qk_dram, v_dram, mixed_dram):
    ident = const["ident"]
    h_tr_hi, h_tr_lo = h_tr
    attn_cols = 3 * D_CONV
    v_first, conv_first = 8, 12
    ahead = 2 * TG

    with ExitStack() as ctx:
        m = Memory(nc, ctx)
        w_raw = [m.sb(f"p_w_raw{i}", [P, KC, P]) for i in range(2)]
        w_hi = [m.sb(f"p_w_hi{i}", [P, KC, P], F32R) for i in range(2)]
        w_lo = [m.sb(f"p_w_lo{i}", [P, KC, P], F32R) for i in range(2)]
        qk_out = [m.sb(f"p_qk_out{i}", [P, 2, BANK], F32R) for i in range(2)]
        v_tr = [m.sb(f"p_v_tr{i}", [P, BANK]) for i in range(2)]
        v_out = [m.sb(f"p_v_out{i}", [P, BANK // P, 2, 2, HEAD_DIM], F32R) for i in range(2)]
        gate_c = m.sb("p_gate_c", [P, SEQ])
        padded = m.sb("p_padded", [P, CONV_K - 1 + SEQ])
        conv = m.sb("p_conv", [P, SEQ])
        taps = m.sb("p_taps", [P, CONV_K, CC])
        conv_out = [m.sb(f"p_conv_out{i}", [P, BANK]) for i in range(2)]
        proj_ps = [m.ps(f"p_proj_ps{i}", [P, BANK]) for i in range(TG)]
        v_ps = [m.ps(f"p_v_ps{i}", [P, BANK // P, 2, HEAD_DIM]) for i in range(2)]

        w_landed = [m.sem(f"p_w_landed{i}") for i in range(2)]
        taps_landed = m.sem("p_taps_landed")
        w_hi_ready, w_lo_ready = m.sem("p_w_hi_ready"), m.sem("p_w_lo_ready")
        projected = m.sem("p_projected")
        taken = m.sem("p_taken")
        qk_hi_ready = m.sem("p_qk_hi_ready")
        qk_sent = [m.sem(f"p_qk_sent{i}") for i in range(2)]
        v_turned = m.sem("p_v_turned")
        v_hi_ready, v_lo_ready = m.sem("p_v_hi_ready"), m.sem("p_v_lo_ready")
        v_sent = [m.sem(f"p_v_sent{i}") for i in range(2)]
        pad_ready = m.sem("p_pad_ready")
        tap_done = m.sem("p_tap_done")
        conv_sent = [m.sem(f"p_conv_sent{i}") for i in range(2)]

        def walk(engine, attn, conv_piece):
            for kind, base in (("q", 0), ("k", 4), ("v", v_first)):
                with engine.Fori(0, 2) as i:
                    for parity in range(2):
                        attn(kind, base + 2 * i + parity, parity, base // 2 + i + 1)
            with engine.Fori(0, CC // 2) as i:
                for half in range(2):
                    for n, part in enumerate((1, 2, 0)):
                        local = 3 * half + n
                        conv_piece(2 * i + half, part, conv_first + 6 * i + local, local % 2,
                                   conv_first // 2 + 3 * i + local // 2 + 1)

        with nc.Block() as block:

            @block.gpsimd
            def _(pool):
                def load(col, chunk, parity):
                    pool.wait_ge(w_lo_ready, chunk + 1)
                    pool.dma_start(w_raw[parity][:], w_in[:, bass.ds(col, P)].rearrange("(k p) c -> p k c", p=P)
                                   ).then_inc(w_landed[parity], 16)

                walk(pool, lambda kind, chunk, parity, use: load(attn_cols + chunk * P, chunk, parity),
                     lambda piece, part, chunk, parity, use: load(part * D_CONV + piece * P, chunk, parity))

            @block.scalar
            def _(act):
                def split(chunk, parity, use):
                    act.wait_ge(w_landed[parity], 16 * use)
                    act.wait_ge(projected, TG * chunk + TG)
                    act.copy(w_hi[parity][:], w_raw[parity][:]).then_inc(w_hi_ready, 1)

                def attn(kind, chunk, parity, use):
                    split(chunk, parity, use)
                    for tg in range(TG):
                        b = tg % 2
                        if kind == "v":
                            step = TG * (chunk - v_first) + tg
                            act.wait_ge(v_turned, step + 3)
                            act.wait_ge(v_sent[b], 32 * (2 * (chunk - v_first) + tg // 2 + 1))
                            act.copy(v_out[b][:, :, :, 0, :], v_ps[b][:]).then_inc(v_hi_ready, 1)
                        else:
                            act.wait_ge(projected, ahead + TG * chunk + tg + 1)
                            act.wait_ge(qk_sent[b], 16 * (2 * chunk + tg // 2 + 1))
                            act.activation(qk_out[b][:, 0, :], proj_ps[tg][:], ACT.Copy,
                                           scale=SCALE if kind == "q" else 1.0).then_inc(qk_hi_ready, 1)

                walk(act, attn, lambda piece, part, chunk, parity, use: split(chunk, parity, use))

            @block.vector
            def _(dve):
                dve.sem_inc(w_lo_ready, 2)
                dve.sem_inc(taken, TG)
                dve.sem_inc(v_lo_ready, 2)
                dve.sem_inc(tap_done, CONV_K)
                dve.memset(padded[:, 0:CONV_K - 1], 0.0).then_inc(pad_ready, 1)

                def split(chunk, parity):
                    dve.wait_ge(w_hi_ready, chunk + 1)
                    dve.tensor_tensor(w_lo[parity][:], w_raw[parity][:], w_hi[parity][:].bitcast(F32), ALU.subtract
                                      ).then_inc(w_lo_ready, 1)

                def attn(kind, chunk, parity, use):
                    split(chunk, parity)

                    def v_low(tg):
                        b, step = tg % 2, TG * (chunk - v_first) + tg
                        dve.wait_ge(v_hi_ready, step + 1)
                        dve.tensor_tensor(v_out[b][:, :, :, 1, :], v_ps[b][:], v_out[b][:, :, :, 0, :].bitcast(F32),
                                          ALU.subtract).then_inc(v_lo_ready, 1)

                    for tg in range(TG):
                        b = tg % 2
                        if kind == "v":
                            dve.wait_ge(projected, ahead + TG * chunk + tg + 1)
                            dve.wait_ge(v_turned, TG * (chunk - v_first) + tg + 1)
                            dve.tensor_copy(v_tr[b][:], proj_ps[tg][:]).then_inc(taken, 1)
                            if tg:
                                v_low(tg - 1)
                        else:
                            dve.wait_ge(qk_hi_ready, TG * chunk + tg + 1)
                            dve.scalar_tensor_tensor(qk_out[b][:, 1, :], proj_ps[tg][:], SCALE if kind == "q" else 1.0,
                                                     qk_out[b][:, 0, :].bitcast(F32), ALU.mult, ALU.subtract
                                                     ).then_inc(taken, 1)
                    if kind == "v":
                        v_low(TG - 1)

                def conv_piece(piece, part, chunk, parity, use):
                    split(chunk, parity)
                    for tg in range(TG):
                        b, cols = tg % 2, slice(tg * BANK, (tg + 1) * BANK)
                        dve.wait_ge(projected, ahead + TG * chunk + tg + 1)
                        if part == 1:
                            dve.wait_ge(taken, TG * chunk + tg + 1)
                            dve.tensor_copy(gate_c[:, cols], proj_ps[tg][:]).then_inc(taken, 1)
                        elif part == 2:
                            dve.wait_ge(taken, TG * (chunk - 1) + TG + tg + 1)
                            if tg == 0:
                                dve.wait_ge(tap_done, CONV_K * (piece + 1))
                            dve.tensor_tensor(padded[:, CONV_K - 1 + tg * BANK:CONV_K - 1 + (tg + 1) * BANK],
                                              proj_ps[tg][:], gate_c[:, cols], ALU.mult).then_inc(taken, 1)
                        else:
                            dve.wait_ge(conv_sent[b], 16 * (2 * piece + tg // 2 + 1))
                            dve.tensor_tensor(conv_out[b][:], proj_ps[tg][:], conv[:, cols], ALU.mult
                                              ).then_inc(taken, 1)
                    if part == 2:
                        dve.wait_ge(taken, TG * (chunk + 2))
                        for n in range(CONV_K):
                            tap = CONV_K - 1 - n
                            if n == 0:
                                dve.tensor_scalar(conv[:], padded[:, tap:tap + SEQ], taps[:, tap, bass.ds(piece, 1)],
                                                  None, ALU.mult).then_inc(tap_done, 1)
                            else:
                                dve.wait_ge(tap_done, CONV_K * (piece + 1) + n)
                                dve.scalar_tensor_tensor(conv[:], padded[:, tap:tap + SEQ],
                                                         taps[:, tap, bass.ds(piece, 1)], conv[:], ALU.mult, ALU.add
                                                         ).then_inc(tap_done, 1)
                        dve.wait_ge(tap_done, CONV_K * (piece + 2))

                dve.wait_ge(taps_landed, 16)
                dve.wait_ge(pad_ready, 1)
                walk(dve, attn, conv_piece)

            @block.sync
            def _(sp):
                sp.dma_start(taps[:], conv_w).then_inc(taps_landed, 16)
                for b in range(2):
                    sp.sem_inc(qk_sent[b], 16)
                    sp.sem_inc(v_sent[b], 32)
                    sp.sem_inc(conv_sent[b], 16)

                def attn(kind, chunk, parity, use):
                    row = sp.snap((chunk - v_first) * 2 if kind == "v" else chunk * P)
                    for tg in range(TG):
                        b, tokens = tg % 2, slice(tg * BANK, (tg + 1) * BANK)
                        if kind == "v":
                            sp.wait_ge(v_lo_ready, TG * (chunk - v_first) + tg + 3)
                            for head in range(2):
                                sp.dma_start(
                                    v_dram[bass.ds(row + head, 1), :, tg * (BANK // P):(tg + 1) * (BANK // P), :
                                           ].rearrange("h p t d -> p (h t) d"),
                                    v_out[b][:, :, head, :, :].rearrange("p t s d -> p t (s d)").bitcast(F32)).then_inc(v_sent[b], 16)
                        else:
                            sp.wait_ge(taken, TG * chunk + tg + 1 + TG)
                            sp.dma_start(qk_dram[:, bass.ds(row, P), tokens].rearrange("s c t -> c s t"),
                                           qk_out[b][:].bitcast(F32)).then_inc(qk_sent[b], 16)

                def conv_piece(piece, part, chunk, parity, use):
                    if part == 0:
                        row = sp.snap(piece * P)
                        for tg in range(TG):
                            b = tg % 2
                            sp.wait_ge(taken, TG * chunk + tg + 1 + TG)
                            sp.dma_start(mixed_dram[bass.ds(row, P), tg * BANK:(tg + 1) * BANK],
                                           conv_out[b][:]).then_inc(conv_sent[b], 16)

                walk(sp, attn, conv_piece)
                for b in range(2):
                    sp.wait_ge(qk_sent[b], 16 * (2 * v_first + 1))
                    sp.wait_ge(v_sent[b], 32 * (2 * CC + 1))
                    sp.wait_ge(conv_sent[b], 16 * (2 * CC + 1))

            @block.tensor
            def _(pe):
                pe.sem_inc(projected, ahead)
                pe.sem_inc(v_turned, 2)

                def product(chunk, parity, tg):
                    pe.wait_ge(taken, TG * chunk + tg + 1)
                    terms = [(k, w, h) for k in range(KC) for w, h in
                             ((w_hi, h_tr_hi), (w_hi, h_tr_lo), (w_lo, h_tr_hi))]
                    for n, (k, w, h) in enumerate(terms):
                        last = pe.matmul(proj_ps[tg][:], w[parity][:, k, :], h[:, k, tg * BANK:(tg + 1) * BANK],
                                         start=n == 0, stop=n == len(terms) - 1)
                    last.then_inc(projected, 1)

                def turn_v(chunk, tg):
                    b, step = tg % 2, TG * (chunk - v_first) + tg
                    pe.wait_ge(taken, TG * chunk + tg + 1 + TG)
                    pe.wait_ge(v_lo_ready, step + 1)
                    for n in range(BANK // P):
                        last = pe.transpose(v_ps[b][:, n, :, :].rearrange("p h d -> p (h d)"),
                                            v_tr[b][:, n * P:(n + 1) * P], ident[:])
                    last.then_inc(v_turned, 1)

                def attn(kind, chunk, parity, use):
                    pe.wait_ge(w_lo_ready, chunk + 3)
                    for tg in range(TG):
                        product(chunk, parity, tg)
                        if kind == "v" and tg:
                            turn_v(chunk, tg - 1)
                    if kind == "v":
                        turn_v(chunk, TG - 1)

                def conv_piece(piece, part, chunk, parity, use):
                    pe.wait_ge(w_lo_ready, chunk + 3)
                    for tg in range(TG):
                        product(chunk, parity, tg)

                walk(pe, attn, conv_piece)


def attend(nc, const, qk_dram, v_dram, mixed_dram):
    queries = BANK
    per_group = queries // P
    steps = []
    for head in range(2):
        for group in range(TG):
            for j in range(per_group * group + per_group - 1, -1, -1):
                steps.append((head, group, j, max(0, j - per_group * group) * P))
    n_steps = len(steps)
    first = [j == per_group * group + per_group - 1 for _, group, j, _ in steps]
    last = [j == 0 for _, _, j, _ in steps]
    diagonal = [j >= per_group * group for _, group, j, _ in steps]
    adds = [0]
    for n in range(n_steps):
        adds.append(adds[-1] + (not last[n]))
    masks, clears = [0], [0]
    for n in range(n_steps):
        masks.append(masks[-1] + diagonal[n])
        clears.append(clears[-1] + (steps[n][3] > 0))
    groups_before = [0]
    for n in range(n_steps):
        groups_before.append(groups_before[-1] + last[n])
    Z, E_BUFS, S_BUFS, T_BUFS, W_BUFS = 6, 3, 4, 4, 3
    SUFFIX_LAG, VALUE_LAG = 3, 6
    LN_LAG, EXP_LAG, EVAC_LAG = 1, 4, 7

    def free(n, size):
        return max(n + 1, size)

    with ExitStack() as ctx:
        m = Memory(nc, ctx)
        keys = [m.sb(f"a_keys{i}", [P, SEQ], F32R) for i in range(2)]
        q_hi = [m.sb(f"a_q_hi{i}", [P, SEQ], F32R) for i in range(2)]
        q_lo = [m.sb(f"a_q_lo{i}", [P, SEQ], F32R) for i in range(2)]
        vals = [m.sb(f"a_vals{i}", [P, TILES, P], F32R) for i in range(2)]
        expz = [m.sb(f"a_expz{i}", [P, BANK]) for i in range(E_BUFS)]
        keep = [m.sb(f"a_keep{i}", [P, BANK]) for i in range(S_BUFS)]
        keep_hi = [m.sb(f"a_keep_hi{i}", [P, BANK], F32R) for i in range(W_BUFS)]
        keep_lo = [m.sb(f"a_keep_lo{i}", [P, BANK], F32R) for i in range(W_BUFS)]
        total = [m.sb(f"a_total{i}", [P, BANK]) for i in range(T_BUFS)]
        wts = [m.sb(f"a_wts{i}", [P, BANK]) for i in range(W_BUFS)]
        wts_hi = [m.sb(f"a_wts_hi{i}", [P, BANK], F32R) for i in range(W_BUFS)]
        wts_lo = [m.sb(f"a_wts_lo{i}", [P, BANK], F32R) for i in range(W_BUFS)]
        tri_f = m.sb("a_tri_f", [P, P])
        tri = m.sb("a_tri", [P, P], F32R)
        square = m.sb("a_square", [P, P])
        mask = m.sb("a_mask", [P, P])
        zero = m.sb("a_zero", [P, P])
        blank_f = m.sb("a_blank_f", [P, BANK])
        blank = m.sb("a_blank", [P, BANK], F32R)
        half_out = [m.sb(f"a_half_out{i}", [HEAD_DIM, BANK]) for i in range(2)]
        head_out = [m.sb(f"a_head_out{i}", [HEAD_DIM, BANK]) for i in range(2)]
        z_ps = [m.ps(f"a_z_ps{i}", [P, BANK]) for i in range(Z)]
        out_ps = [m.ps(f"a_out_ps{i}", [P, BANK]) for i in range(2)]

        head_landed = [m.sem(f"a_head_landed{i}") for i in range(2)]
        const_ready = m.sem("a_const_ready")
        tri_ready = m.sem("a_tri_ready")
        z_ready = m.sem("a_z_ready")
        exp_ready, capped, ln_ready = m.sem("a_exp_ready"), m.sem("a_capped"), m.sem("a_ln_ready")
        keep_raw = m.sem("a_keep_raw")
        keep_masked = m.sem("a_keep_masked")
        keep_hi_ready, keep_lo_ready = m.sem("a_keep_hi_ready"), m.sem("a_keep_lo_ready")
        total_cleared, total_ready = m.sem("a_total_cleared"), m.sem("a_total_ready")
        suffix_ready = m.sem("a_suffix_ready")
        wts_raw, wts_masked = m.sem("a_wts_raw"), m.sem("a_wts_masked")
        wts_hi_ready, wts_lo_ready = m.sem("a_wts_hi_ready"), m.sem("a_wts_lo_ready")
        valued = m.sem("a_valued")
        half_ready, out_ready = m.sem("a_half_ready"), m.sem("a_out_ready")
        out_sent = [m.sem(f"a_out_sent{i}") for i in range(2)]
        rounds = HEADS // 2

        with nc.Block() as block:

            @block.sync
            def _(sp):
                for b in range(2):
                    sp.sem_inc(out_sent[b], 16)

                def stage_in(r, b):
                    head = sp.snap(2 * r + b) if not isinstance(r, int) else 2 * r + b
                    for part in range(2):
                        rows = slice(part * HEAD_DIM, (part + 1) * HEAD_DIM)
                        k_rows, q_rows = bass.ds(D_ATTN + head * HEAD_DIM, HEAD_DIM), bass.ds(head * HEAD_DIM, HEAD_DIM)
                        for dst, src in ((keys, qk_dram[part, k_rows, :]), (q_hi, qk_dram[0, q_rows, :]),
                                         (q_lo, qk_dram[1, q_rows, :])):
                            sp.dma_start(dst[b][rows, :].bitcast(F32), src).then_inc(head_landed[b], 16)
                    sp.dma_start(vals[b][:].bitcast(F32), v_dram[bass.ds(head, 1), :, :, :].rearrange(
                        "h p t d -> p (h t) d")).then_inc(head_landed[b], 16)

                def send_head(r, b):
                    for group in range(TG):
                        n = TG * b + group
                        row = sp.snap(D_CONV + (2 * r + b) * HEAD_DIM)
                        sp.wait_ge(out_ready, 2 * TG * r + n + 2)
                        sp.dma_start(mixed_dram[bass.ds(row, HEAD_DIM), group * BANK:(group + 1) * BANK],
                                     head_out[n % 2][:]).then_inc(out_sent[n % 2], 16)

                stage_in(0, 0)
                stage_in(0, 1)
                with sp.Fori(0, rounds - 1) as r:
                    for b in range(2):
                        send_head(r, b)
                        stage_in(r + 1, b)
                for b in range(2):
                    for group in range(TG):
                        n = TG * b + group
                        row = D_CONV + (2 * (rounds - 1) + b) * HEAD_DIM
                        sp.wait_ge(out_ready, 2 * TG * (rounds - 1) + n + 2)
                        sp.dma_start(mixed_dram[row:row + HEAD_DIM, group * BANK:(group + 1) * BANK],
                                     head_out[n % 2][:]).then_inc(out_sent[n % 2], 16)
                for b in range(2):
                    sp.wait_ge(out_sent[b], 16 * (TG * rounds + 1))

            @block.gpsimd
            def _(pool):
                pool.memset(square[:], -1.0).then_inc(const_ready, 1)
                pool.memset(tri_f[:], -1.0).then_inc(const_ready, 1)
                pool.memset(mask[:], 1.0).then_inc(const_ready, 1)
                pool.memset(zero[:], 0.0).then_inc(const_ready, 1)
                pool.memset(blank_f[:], 0.0).then_inc(const_ready, 1)
                pool.wait_ge(const_ready, 5)
                pool.affine_select(out=tri_f[:], in_=tri_f[:], compare_op=ALU.is_ge, fill=0.0, base=0,
                                   pattern=[[-1, P]], channel_multiplier=1).then_inc(const_ready, 1)
                pool.affine_select(out=mask[:], in_=mask[:], compare_op=ALU.is_gt, fill=0.0, base=0,
                                   pattern=[[1, P]], channel_multiplier=-1).then_inc(const_ready, 1)
                pool.sem_inc(total_ready, 1)
                with pool.Fori(0, rounds) as r:
                    for n, (_, _, _, lo) in enumerate(steps):
                        if last[n]:
                            continue
                        dst, src = total[(n + 1) % T_BUFS], total[n % T_BUFS]
                        pool.wait_ge(suffix_ready, n_steps * r + max(n + 1 - T_BUFS + 2, 1))
                        if lo:
                            pool.tensor_tensor(dst[:, lo - P:lo], zero[:], zero[:], ALU.add).then_inc(total_cleared, 1)
                            pool.wait_ge(total_cleared, clears[-1] * r + clears[n] + 1)
                        pool.wait_ge(keep_raw, E_BUFS + n_steps * r + n + 1)
                        if diagonal[n]:
                            pool.wait_ge(keep_masked, masks[-1] * r + masks[n] + 1)
                        if first[n]:
                            pool.tensor_tensor(dst[:, lo:], keep[n % S_BUFS][:, lo:], zero[:], ALU.add
                                               ).then_inc(total_ready, 1)
                        else:
                            pool.wait_ge(total_ready, adds[-1] * r + adds[n] + 1)
                            pool.tensor_tensor(dst[:, lo:], src[:, lo:], keep[n % S_BUFS][:, lo:], ALU.add
                                               ).then_inc(total_ready, 1)

            @block.scalar
            def _(act):
                act.wait_ge(const_ready, 7)
                act.copy(tri[:], tri_f[:]).then_inc(tri_ready, 1)
                act.copy(blank[:], blank_f[:]).then_inc(tri_ready, 1)
                with act.Fori(0, rounds) as r:
                    act.preload_act_table_set("natural_log_exp_and_others")
                    base = n_steps * r
                    for slot in range(n_steps + EVAC_LAG):
                        n = slot
                        if n < n_steps:
                            lo = steps[n][3]
                            act.wait_ge(z_ready, base + n + 1)
                            act.wait_ge(keep_raw, base + free(n, E_BUFS))
                            act.activation(expz[n % E_BUFS][:, lo:], z_ps[n % Z][:, lo:], ACT.Exp
                                           ).then_inc(exp_ready, 1)
                        n = slot - EXP_LAG
                        if 0 <= n < n_steps:
                            lo = steps[n][3]
                            act.wait_ge(suffix_ready, base + n + 2)
                            act.wait_ge(wts_lo_ready, base + free(n, W_BUFS))
                            act.activation(wts[n % W_BUFS][:, lo:], z_ps[n % Z][:, lo:], ACT.Exp).then_inc(wts_raw, 1)
                        n = slot - LN_LAG
                        if 0 <= n < n_steps:
                            lo = steps[n][3]
                            act.wait_ge(capped, base + n + 1)
                            act.activation(expz[n % E_BUFS][:, lo:], expz[n % E_BUFS][:, lo:], ACT.Ln, bias=1.0
                                           ).then_inc(ln_ready, 1)
                        n = slot - EXP_LAG - 1
                        if 0 <= n < n_steps:
                            lo = steps[n][3]
                            act.wait_ge(wts_raw, base + n + 1)
                            if diagonal[n]:
                                act.wait_ge(wts_masked, masks[-1] * r + masks[n] + 1)
                            act.wait_ge(valued, base + free(n, W_BUFS))
                            act.copy(wts_hi[n % W_BUFS][:, lo:], wts[n % W_BUFS][:, lo:]).then_inc(wts_hi_ready, 1)
                        n = slot - EVAC_LAG
                        if 0 <= n < n_steps and last[n]:
                            g = groups_before[n]
                            act.wait_ge(valued, base + n + 1 + W_BUFS)
                            act.wait_ge(out_ready, 2 * TG * r + max(g, 1))
                            act.copy(half_out[g % 2][:], out_ps[g % 2][HEAD_DIM:, :]).then_inc(half_ready, 1)

            @block.vector
            def _(dve):
                dve.sem_inc(keep_raw, E_BUFS)
                dve.sem_inc(out_ready, 1)
                dve.sem_inc(wts_lo_ready, W_BUFS)
                with dve.Fori(0, rounds) as r:
                    base = n_steps * r
                    for slot in range(n_steps + EVAC_LAG):
                        n = slot
                        if n < n_steps:
                            lo = steps[n][3]
                            dve.wait_ge(exp_ready, base + n + 1)
                            dve.tensor_scalar(expz[n % E_BUFS][:, lo:], expz[n % E_BUFS][:, lo:], EXP_CAP, None,
                                              ALU.min).then_inc(capped, 1)
                        n = slot - LN_LAG
                        if 0 <= n < n_steps:
                            lo, s, w = steps[n][3], keep[n % S_BUFS], n % W_BUFS
                            dve.wait_ge(ln_ready, base + n + 1)
                            if n >= S_BUFS:
                                dve.wait_ge(total_ready, adds[-1] * r + adds[n - S_BUFS + 1] + 1)
                            else:
                                dve.wait_ge(total_ready, adds[-1] * r + 1)
                            dve.tensor_tensor(s[:, lo:], z_ps[n % Z][:, lo:], expz[n % E_BUFS][:, lo:], ALU.max
                                              ).then_inc(keep_raw, 1)
                        n = slot - EXP_LAG
                        if 0 <= n < n_steps and diagonal[n]:
                            lo, w = steps[n][3], n % W_BUFS
                            dve.wait_ge(wts_raw, base + n + 1)
                            dve.scalar_tensor_tensor(wts[w][:, lo:lo + P], wts[w][:, lo:lo + P], 2.0, mask[:],
                                                     ALU.min, ALU.mult).then_inc(wts_masked, 1)
                        n = slot - LN_LAG
                        if 0 <= n < n_steps:
                            lo, s, w = steps[n][3], keep[n % S_BUFS], n % W_BUFS
                            dve.wait_ge(keep_raw, base + E_BUFS + n + 1)
                            if diagonal[n]:
                                dve.tensor_tensor(s[:, lo:lo + P], s[:, lo:lo + P], mask[:], ALU.mult
                                                  ).then_inc(keep_masked, 1)
                                dve.wait_ge(keep_masked, masks[-1] * r + masks[n] + 1)
                            dve.wait_ge(suffix_ready, base + max(n + 2 - W_BUFS, 1))
                            dve.tensor_copy(keep_hi[w][:, lo:], s[:, lo:]).then_inc(keep_hi_ready, 1)
                        n = slot - EXP_LAG - 1
                        if 0 <= n < n_steps:
                            lo, w = steps[n][3], n % W_BUFS
                            dve.wait_ge(wts_hi_ready, base + n + 1)
                            dve.tensor_tensor(wts_lo[w][:, lo:], wts[w][:, lo:], wts_hi[w][:, lo:].bitcast(F32),
                                              ALU.subtract).then_inc(wts_lo_ready, 1)
                        n = slot - LN_LAG
                        if 0 <= n < n_steps:
                            lo, s, w = steps[n][3], keep[n % S_BUFS], n % W_BUFS
                            dve.wait_ge(keep_hi_ready, base + n + 1)
                            dve.tensor_tensor(keep_lo[w][:, lo:], s[:, lo:], keep_hi[w][:, lo:].bitcast(F32),
                                              ALU.subtract).then_inc(keep_lo_ready, 1)
                        n = slot - EVAC_LAG
                        if 0 <= n < n_steps and last[n]:
                            g = groups_before[n]
                            dve.wait_ge(half_ready, 2 * TG * r + g + 1)
                            dve.wait_ge(out_sent[g % 2], 16 * (TG * r + g // 2 + 1))
                            dve.tensor_tensor(head_out[g % 2][:], out_ps[g % 2][:HEAD_DIM, :], half_out[g % 2][:],
                                              ALU.add).then_inc(out_ready, 1)

            @block.tensor
            def _(pe):
                pe.sem_inc(suffix_ready, 1)
                pe.sem_inc(valued, W_BUFS)
                pe.wait_ge(tri_ready, 2)
                with pe.Fori(0, rounds) as r:
                    base = n_steps * r
                    for slot in range(n_steps + VALUE_LAG):
                        n = slot
                        if n < n_steps:
                            b, group, j, lo = steps[n]
                            cols = slice(group * BANK + lo, (group + 1) * BANK)
                            if j == per_group - 1 and group == 0:
                                pe.wait_ge(head_landed[b], 7 * 16 * (r + 1))
                            if n >= Z:
                                pe.wait_ge(wts_raw, base + n + 1 - Z)
                            for i, q in enumerate((q_hi, q_lo)):
                                mm = pe.matmul(z_ps[n % Z][:, lo:], keys[b][:, j * P:(j + 1) * P], q[b][:, cols],
                                               start=i == 0, stop=i == 1)
                            mm.then_inc(z_ready, 1)
                        n = slot - SUFFIX_LAG
                        if 0 <= n < n_steps:
                            lo, w = steps[n][3], n % W_BUFS
                            if not first[n]:
                                skip = P if diagonal[n] else 0
                                pe.wait_ge(total_ready, adds[-1] * r + adds[n] + 1)
                                pe.wait_ge(keep_raw, E_BUFS + base + n + 1)
                                pe.matmul(z_ps[n % Z][:, lo + skip:], square[:], total[n % T_BUFS][:, lo + skip:],
                                          start=False, stop=False, skip_group_check=True)
                            pe.wait_ge(keep_lo_ready, base + n + 1)
                            pe.matmul(z_ps[n % Z][:, lo:], tri[:], keep_hi[w][:, lo:], start=False, stop=False,
                                      skip_group_check=True)
                            pe.matmul(z_ps[n % Z][:, lo:], tri[:], keep_lo[w][:, lo:], start=False, stop=True,
                                      skip_group_check=True).then_inc(suffix_ready, 1)
                        n = slot - VALUE_LAG
                        if 0 <= n < n_steps:
                            b, group, j, lo = steps[n]
                            w, g = n % W_BUFS, groups_before[n]
                            if first[n]:
                                pe.wait_ge(out_ready, 2 * TG * r + max(g, 1))
                                pe.matmul(out_ps[g % 2][:], tri[:], blank[:], start=True, stop=False)
                            pe.wait_ge(wts_lo_ready, base + n + 1 + W_BUFS)
                            pe.matmul(out_ps[g % 2][:, lo:], vals[b][:, j, :], wts_hi[w][:, lo:], start=False,
                                      stop=False)
                            pe.matmul(out_ps[g % 2][:, lo:], vals[b][:, j, :], wts_lo[w][:, lo:], start=False,
                                      stop=last[n]).then_inc(valued, 1)


def mix(nc, const, logits, w_out, g_mix, ln_g, ln_b, router_w, h_dram, mixed_dram, h1_dram):
    ident = const["ident"]
    with ExitStack() as ctx:
        m = Memory(nc, ctx)
        w_raw = m.sb("m_w_raw", [P, KC, D])
        w_hi, w_lo = m.sb("m_w_hi", [P, KC, D], F32R), m.sb("m_w_lo", [P, KC, D], F32R)
        row_gain = m.sb("m_row_gain", [P, KC])
        gain, shift = m.sb("m_gain", [P, D]), m.sb("m_shift", [P, D])
        router = m.sb("m_router", [P, KC, EXPERTS])
        ones = m.sb("m_ones", [P, 1])
        eps = m.sb("m_eps", [P, 2])
        ch_raw = [m.sb(f"m_ch_raw{i}", [P, KC, P]) for i in range(2)]
        ch_hi = [m.sb(f"m_ch_hi{i}", [P, KC, P], F32R) for i in range(2)]
        ch_lo = [m.sb(f"m_ch_lo{i}", [P, KC, P], F32R) for i in range(2)]
        square = [m.sb(f"m_square{i}", [P, KC, P]) for i in range(2)]
        rows = [m.sb(f"m_rows{i}", [P, D]) for i in range(2)]
        h1_tr = m.sb("m_h1_tr", [P, KC, P])
        rms = m.sb("m_rms", [P, 2])
        stats, moments = m.sb("m_stats", [P, 2, 6]), m.sb("m_moments", [P, 2])
        rstd, offset = m.sb("m_rstd", [P, 1]), m.sb("m_offset", [P, 1])
        conv_ps, attn_ps = m.ps("m_conv_ps", [P, D]), m.ps("m_attn_ps", [P, D])
        tr_ps = m.ps("m_tr_ps", [P, KC, P])
        rms_ps = m.ps("m_rms_ps", [P, BANK])
        logit_ps = m.ps("m_logit_ps", [P, BANK])

        w_landed, params_landed = m.sem("m_w_landed"), m.sem("m_params_landed")
        w_gained, w_hi_ready, w_lo_ready = m.sem("m_w_gained"), m.sem("m_w_hi_ready"), m.sem("m_w_lo_ready")
        const_ready = m.sem("m_const_ready")
        ch_landed = [m.sem(f"m_ch_landed{i}") for i in range(2)]
        h_landed = [m.sem(f"m_h_landed{i}") for i in range(2)]
        h1_sent = [m.sem(f"m_h1_sent{i}") for i in range(2)]
        ch_hi_ready, ch_lo_ready, squared = m.sem("m_ch_hi_ready"), m.sem("m_ch_lo_ready"), m.sem("m_squared")
        res_scaled = m.sem("m_res_scaled")
        rms_summed, conv_ready, attn_ready = m.sem("m_rms_summed"), m.sem("m_conv_ready"), m.sem("m_attn_ready")
        rms_root, rms_ready = m.sem("m_rms_root"), m.sem("m_rms_ready")
        conv_added, attn_added = m.sem("m_conv_added"), m.sem("m_attn_added")
        half_stats, stats_seen, moments_ready = m.sem("m_half_stats"), m.sem("m_stats_seen"), m.sem("m_moments_ready")
        std_ready, rstd_ready, offset_ready = m.sem("m_std_ready"), m.sem("m_rstd_ready"), m.sem("m_offset_ready")
        scaled, gained, h1_ready = m.sem("m_scaled"), m.sem("m_gained"), m.sem("m_h1_ready")
        transposed, tr_copied = m.sem("m_transposed"), m.sem("m_tr_copied")
        logits_summed, logits_copied = m.sem("m_logits_summed"), m.sem("m_logits_copied")
        half = KC // 2

        with nc.Block() as block:

            @block.sync
            def _(sp):
                for b in range(2):
                    sp.sem_inc(h1_sent[b], 16)
                sp.dma_start(row_gain[:], g_mix).then_inc(params_landed, 16)
                sp.dma_start(router[:], router_w.rearrange("(k p) e -> p k e", p=P)).then_inc(params_landed, 16)
                load_row(sp, gain[:], ln_g, params_landed)
                load_row(sp, shift[:], ln_b, params_landed)
                sp.dma_start(w_raw[:], w_out.rearrange("(k p) n -> p k n", p=P)).then_inc(w_landed, 16)

                def at(t):
                    return t * P if isinstance(t, int) else sp.snap(t * P)

                def load_channels(t, b, use):
                    tokens = at(t)
                    sp.wait_ge(ch_lo_ready, t + 1)
                    sp.wait_ge(squared, t + 1)
                    sp.dma_start(ch_raw[b][:], mixed_dram[:, bass.ds(tokens, P)].rearrange("(k p) t -> p k t", p=P)
                                 ).then_inc(ch_landed[b], 16)

                def load_residual(t, b, use):
                    tokens = at(t)
                    sp.wait_ge(h1_sent[b], 16 * use + 16)
                    sp.wait_ge(transposed, t + 1)
                    sp.dma_start(rows[b][:], h_dram[bass.ds(tokens, P), :]).then_inc(h_landed[b], 16)

                def send(t, b, use):
                    tokens = at(t)
                    sp.wait_ge(h1_ready, t + 1)
                    sp.dma_start(h1_dram[bass.ds(tokens, P), :], rows[b][:]).then_inc(h1_sent[b], 16)

                skewed(sp, (0, load_channels), (1, load_residual), (2, send))
                for b in range(2):
                    sp.wait_ge(h1_sent[b], 16 * (TILES // 2 + 1))

            @block.gpsimd
            def _(pool):
                pool.memset(ones[:], 1.0).then_inc(const_ready, 1)
                pool.memset(eps[:, 0:1], RMS_EPS).then_inc(const_ready, 1)
                pool.memset(eps[:, 1:2], LN_EPS).then_inc(const_ready, 1)
                pool.wait_ge(params_landed, 64)

                def add_shift(t, b, use):
                    pool.wait_ge(gained, t + 1)
                    pool.tensor_tensor(rows[b][:], rows[b][:], shift[:], ALU.add).then_inc(h1_ready, 1)

                skewed(pool, (1, add_shift))

            @block.scalar
            def _(act):
                act.preload_act_table_set("sqrt_and_others")
                act.wait_ge(const_ready, 3)
                for k in range(KC):
                    act.wait_ge(w_gained, k + 1)
                    act.copy(w_hi[:, k, :], w_raw[:, k, :]).then_inc(w_hi_ready, 1)

                act.sem_inc(squared, 2)
                act.sem_inc(rms_root, 1)
                act.sem_inc(tr_copied, 1)
                act.sem_inc(logits_copied, 1)

                def split(t, b, use):
                    act.wait_ge(ch_landed[b], 16 * use + 16)
                    act.wait_ge(attn_ready, t + 1)
                    act.activation(square[b][:], ch_raw[b][:], ACT.Square).then_inc(squared, 1)
                    act.copy(ch_hi[b][:], ch_raw[b][:]).then_inc(ch_hi_ready, 1)

                def scale_residual(t, b, use):
                    act.wait_ge(h_landed[b], 16 * use + 16)
                    act.mul(rows[b][:], rows[b][:], ALPHA).then_inc(res_scaled, 1)

                def normalise(t, b, use):
                    act.wait_ge(rms_summed, t + 1)
                    act.wait_ge(attn_added, t + 1)
                    act.activation(rms[:], rms_ps[:, 0:2], ACT.Sqrt, scale=1.0 / D_CONV, bias=eps[:, 0:1]
                                   ).then_inc(rms_root, 1)
                    act.wait_ge(moments_ready, t + 1)
                    act.activation(rstd[:], moments[:, 1:2], ACT.Sqrt, bias=eps[:, 1:2]).then_inc(std_ready, 1)
                    act.wait_ge(offset_ready, t + 1)
                    act.activation(rows[b][:], rows[b][:], ACT.Identity, scale=rstd[:], bias=offset[:]
                                   ).then_inc(scaled, 1)

                def copy_transpose(t, b, use):
                    act.wait_ge(transposed, t + 3)
                    act.wait_ge(logits_summed, t + 1)
                    act.copy(h1_tr[:], tr_ps[:]).then_inc(tr_copied, 1)

                def copy_logits(t, b, use):
                    act.wait_ge(logits_summed, t + 2)
                    act.copy(logits[:, bass.ds(t, 1), :].rearrange("p t e -> p (t e)"), logit_ps[:, 0:EXPERTS]
                             ).then_inc(logits_copied, 1)

                skewed(act, (0, split), (1, scale_residual), (1, normalise), (2, copy_transpose), (3, copy_logits))

            @block.vector
            def _(dve):
                dve.sem_inc(ch_lo_ready, 2)
                dve.sem_inc(attn_added, 1)
                dve.sem_inc(conv_added, 1)
                dve.wait_ge(params_landed, 64)
                dve.wait_ge(w_landed, 16)
                for k in range(KC):
                    dve.tensor_scalar(w_raw[:, k, :], w_raw[:, k, :], row_gain[:, k:k + 1], None, ALU.mult
                                      ).then_inc(w_gained, 1)
                    if k:
                        dve.wait_ge(w_hi_ready, k)
                        dve.tensor_tensor(w_lo[:, k - 1, :], w_raw[:, k - 1, :], w_hi[:, k - 1, :].bitcast(F32),
                                          ALU.subtract).then_inc(w_lo_ready, 1)
                dve.wait_ge(w_hi_ready, KC)
                dve.tensor_tensor(w_lo[:, KC - 1, :], w_raw[:, KC - 1, :], w_hi[:, KC - 1, :].bitcast(F32),
                                  ALU.subtract).then_inc(w_lo_ready, 1)

                def split(t, b, use):
                    dve.wait_ge(ch_hi_ready, t + 1)
                    dve.tensor_tensor(ch_lo[b][:], ch_raw[b][:], ch_hi[b][:].bitcast(F32), ALU.subtract
                                      ).then_inc(ch_lo_ready, 1)

                def normalise(t, b, use):
                    dve.wait_ge(rms_root, t + 2)
                    dve.reciprocal(rms[:], rms[:]).then_inc(rms_ready, 1)
                    dve.wait_ge(rms_ready, t + 1)
                    dve.wait_ge(res_scaled, t + 1)
                    dve.wait_ge(conv_ready, t + 1)
                    dve.scalar_tensor_tensor(rows[b][:], conv_ps[:], rms[:, 0:1], rows[b][:], ALU.mult, ALU.add
                                             ).then_inc(conv_added, 1)
                    dve.wait_ge(conv_added, t + 2)
                    dve.wait_ge(attn_ready, t + 3)
                    dve.scalar_tensor_tensor(rows[b][:], attn_ps[:], rms[:, 1:2], rows[b][:], ALU.mult, ALU.add
                                             ).then_inc(attn_added, 1)
                    dve.wait_ge(attn_added, t + 2)
                    for n in range(2):
                        dve.bn_stats(stats[:, n, :], rows[b][:, n * BANK:(n + 1) * BANK]).then_inc(half_stats, 1)
                    dve.wait_ge(half_stats, 2 * t + 2)
                    dve.sem_inc(stats_seen, 1)
                    dve.bn_aggr(moments[:], stats[:]).then_inc(moments_ready, 1)
                    dve.wait_ge(std_ready, t + 1)
                    dve.reciprocal(rstd[:], rstd[:]).then_inc(rstd_ready, 1)
                    dve.wait_ge(rstd_ready, t + 1)
                    dve.scalar_tensor_tensor(offset[:], moments[:, 0:1], -1.0, rstd[:], ALU.mult, ALU.mult
                                             ).then_inc(offset_ready, 1)
                    dve.wait_ge(scaled, t + 1)
                    dve.tensor_tensor(rows[b][:], rows[b][:], gain[:], ALU.mult).then_inc(gained, 1)

                skewed(dve, (0, split), (1, normalise))

            @block.tensor
            def _(pe):
                pe.sem_inc(attn_ready, 2)
                pe.sem_inc(transposed, 2)
                pe.sem_inc(logits_summed, 1)
                pe.wait_ge(const_ready, 3)
                pe.wait_ge(w_lo_ready, KC)

                def product(out, b, first, bank):
                    terms = [(k, c, w) for k in range(first, first + half) for c, w in
                             ((ch_hi, w_hi), (ch_hi, w_lo), (ch_lo, w_hi))]
                    for n, (k, c, w) in enumerate(terms):
                        mm = pe.matmul(out[:, bank * BANK:(bank + 1) * BANK], c[b][:, k, :],
                                       w[:, k, bank * BANK:(bank + 1) * BANK], start=n == 0, stop=n == len(terms) - 1)
                    return mm

                def products(t, b, use):
                    pe.wait_ge(squared, t + 3)
                    pe.wait_ge(rms_root, t + 1)
                    for side in range(2):
                        for k in range(half):
                            mm = pe.matmul(rms_ps[:, side:side + 1], square[b][:, side * half + k, :], ones[:],
                                           start=k == 0, stop=k == half - 1)
                    mm.then_inc(rms_summed, 1)
                    pe.wait_ge(ch_lo_ready, t + 3)
                    pe.wait_ge(conv_added, t + 1)
                    for bank in range(2):
                        mm = product(conv_ps, b, 0, bank)
                    mm.then_inc(conv_ready, 1)
                    pe.wait_ge(attn_added, t + 1)
                    for bank in range(2):
                        mm = product(attn_ps, b, half, bank)
                    mm.then_inc(attn_ready, 1)

                def transpose(t, b, use):
                    pe.wait_ge(h1_ready, t + 1)
                    pe.wait_ge(tr_copied, t + 1)
                    for k in range(KC):
                        mm = pe.transpose(tr_ps[:, k, :], rows[b][:, k * P:(k + 1) * P], ident[:])
                    mm.then_inc(transposed, 1)

                def route_logits(t, b, use):
                    pe.wait_ge(tr_copied, t + 2)
                    pe.wait_ge(logits_copied, t + 1)
                    for k in range(KC):
                        mm = pe.matmul(logit_ps[:, 0:EXPERTS], h1_tr[:, k, :], router[:, k, :], start=k == 0,
                                       stop=k == KC - 1)
                    mm.then_inc(logits_summed, 1)

                skewed(pe, (1, products), (3, route_logits), (2, transpose))


def route(nc, logits, weight, position_id, first_block, blocks_of, idle_blocks, router_b, slot_dram):
    with ExitStack() as ctx:
        m = Memory(nc, ctx)
        by_expert = [P, TILES, EXPERTS]
        n_groups = TILES * GROUPS
        score, select, bias = m.sb("r_score", by_expert), m.sb("r_select", by_expert), m.sb("r_bias", [P, EXPERTS])
        high = m.sb("r_high", [P, n_groups, 2])
        low = m.sb("r_low", [P, n_groups, 2])
        top = m.sb("r_top", [P, TILES, GROUPS])
        second = m.sb("r_second", [P, TILES, GROUPS])
        group_mask = m.sb("r_group_mask", [P, TILES, GROUPS])
        best = m.sb("r_best", [P, TILES])
        product = m.sb("r_product", by_expert)
        in_group = m.sb("r_in_group", [P, TILES, PER_GROUP])
        group_score = m.sb("r_group_score", [P, TILES, PER_GROUP])
        local = [m.sb(f"r_local{i}", [P, TILES, PER_GROUP]) for i in range(TOP_K)]
        scratch = m.sb("r_scratch", [P, TILES, PER_GROUP])
        chosen = [m.sb(f"r_chosen{i}", by_expert) for i in range(TOP_K)]
        either = m.sb("r_either", by_expert)
        rank = m.sb("r_rank", by_expert)
        before = m.sb("r_before", [P, TILES + 1, EXPERTS])
        over = m.sb("r_over", [P, EXPERTS, TILES])
        n_blocks, ends = m.sb("r_n_blocks", [P, EXPERTS]), m.sb("r_ends", [P, EXPERTS])
        falling = m.sb("r_falling", [P, GROUPS])
        falling_i = m.sb("r_falling_i", [P, GROUPS], I32)
        steps_i, steps = m.sb("r_steps_i", [P, TILES], I32), m.sb("r_steps", [P, TILES])
        ones, tri = m.sb("r_ones", [P, P]), m.sb("r_tri", [P, P])
        token_id = m.sb("r_token_id", [P, TILES], I32)
        position = [m.sb(f"r_position{k}", [P, TILES]) for k in range(TOP_K)]
        table_id = [m.sb(f"r_table_id{k}", [P, TILES], I32) for k in range(TOP_K)]
        block_id = m.sb("r_block_id", [P, TILES], I32)
        none = m.sb("r_none", [P, SLOT_BLOCKS], I32)
        rank_ps, count_ps = m.ps("r_rank_ps", by_expert), m.ps("r_count_ps", by_expert)

        bias_landed = m.sem("r_bias_landed")
        exp_ready = m.sem("r_exp_ready")
        chain = m.sem("r_chain")
        chosen_ready = m.sem("r_chosen_ready")
        counted = m.sem("r_counted")
        routed = m.sem("r_routed")
        pool_const = m.sem("r_pool_const")
        cleared = m.sem("r_cleared")
        scattered = m.sem("r_scattered")

        with nc.Block() as block:

            @block.sync
            def _(sp):
                load_row(sp, bias[:], router_b, bias_landed)

            @block.scalar
            def _(act):
                act.activation(score[:], logits[:], ACT.Exp, scale=-1.0).then_inc(exp_ready, 1)

            @block.gpsimd
            def _(pool):
                pool.iota(falling_i[:], [[-1, GROUPS]], base=GROUPS, channel_multiplier=0).then_inc(pool_const, 1)
                pool.iota(steps_i[:], [[P, TILES]], base=0, channel_multiplier=0).then_inc(pool_const, 1)
                pool.iota(token_id[:], [[P, TILES]], base=0, channel_multiplier=1).then_inc(pool_const, 1)
                pool.memset(ones[:], 1.0).then_inc(pool_const, 1)
                pool.memset(none[:], 0).then_inc(pool_const, 1)
                pool.memset(tri[:], 1.0).then_inc(pool_const, 1)
                pool.wait_ge(pool_const, 6)
                pool.affine_select(out=tri[:], in_=tri[:], compare_op=ALU.is_gt, fill=0.0, base=0,
                                   pattern=[[1, P]], channel_multiplier=-1).then_inc(pool_const, 1)
                pool.dma_start(slot_dram.rearrange("(p b) o -> p (b o)", b=SLOT_BLOCKS), none[:]).then_inc(cleared, 16)
                pool.wait_ge(cleared, 16)
                pool.wait_ge(routed, 1)
                n = 0
                for t in range(TILES):
                    for k in range(TOP_K):
                        pool.indirect_dma_start(
                            out=slot_dram, out_offset=bass.IndirectOffsetOnAxis(ap=table_id[k][:, t:t + 1], axis=0),
                            in_=token_id[:, t:t + 1], in_offset=None).then_inc(scattered, 16)
                        n += 16
                pool.wait_ge(scattered, n)

            @block.tensor
            def _(pe):
                pe.wait_ge(pool_const, 7)
                pe.wait_ge(chosen_ready, 1)
                pe.matmul(rank_ps[:], tri[:], either[:], start=True, stop=True)
                pe.matmul(count_ps[:], ones[:], either[:], start=True, stop=True).then_inc(counted, 1)

            @block.vector
            def _(dve):
                made = [0]

                def step(instruction):
                    made[0] += 1
                    instruction.then_inc(chain, 1)
                    dve.wait_ge(chain, made[0])

                def first_best(out, values, width):
                    shape = [P, TILES, width]
                    step(dve.tensor_reduce(best[:], values[:], AX.X, ALU.max))
                    step(dve.tensor_tensor(out[:], values[:], best[:].unsqueeze(2).to_broadcast(shape), ALU.is_ge))
                    step(dve.tensor_tensor(out[:], out[:], falling[:, GROUPS - width:].unsqueeze(1).to_broadcast(shape),
                                           ALU.mult))
                    step(dve.tensor_reduce(best[:], out[:], AX.X, ALU.max))
                    step(dve.tensor_tensor(out[:], out[:], best[:].unsqueeze(2).to_broadcast(shape), ALU.is_equal))

                dve.wait_ge(exp_ready, 1)
                step(dve.tensor_scalar(score[:], score[:], 1.0, None, ALU.add))
                step(dve.reciprocal(score[:], score[:]))
                dve.wait_ge(bias_landed, 16)
                step(dve.tensor_tensor(select[:], score[:], bias[:].unsqueeze(1).to_broadcast(by_expert), ALU.add))
                dve.wait_ge(pool_const, 7)
                step(dve.tensor_copy(falling[:], falling_i[:]))
                step(dve.tensor_copy(steps[:], steps_i[:]))
                four = select[:].rearrange("p t (g a b) -> p (t g) a b", a=2, b=2)
                step(dve.tensor_tensor(high[:], four[:, :, :, 0], four[:, :, :, 1], ALU.max))
                step(dve.tensor_tensor(low[:], four[:, :, :, 0], four[:, :, :, 1], ALU.min))
                flat = [x[:].rearrange("p t g -> p (t g)") for x in (top, second)]
                step(dve.tensor_tensor(flat[0], high[:, :, 0], high[:, :, 1], ALU.max))
                step(dve.tensor_tensor(flat[1], high[:, :, 0], high[:, :, 1], ALU.min))
                step(dve.tensor_tensor(low[:, :, 0], low[:, :, 0], low[:, :, 1], ALU.max))
                step(dve.tensor_tensor(flat[1], flat[1], low[:, :, 0], ALU.max))
                step(dve.tensor_tensor(top[:], top[:], second[:], ALU.add))
                first_best(group_mask, top, GROUPS)
                by_group = [P, TILES, GROUPS, PER_GROUP]
                mask4 = group_mask[:].unsqueeze(3).to_broadcast(by_group)
                for out, values in ((in_group, select), (group_score, score)):
                    split = values[:].rearrange("p t (g k) -> p t g k", k=PER_GROUP)
                    step(dve.tensor_tensor(product[:].rearrange("p t (g k) -> p t g k", k=PER_GROUP), split, mask4,
                                           ALU.mult))
                    step(dve.tensor_reduce(out[:], product[:].rearrange("p t (g k) -> p t k g", k=PER_GROUP), AX.X,
                                           ALU.add))
                first_best(local[0], in_group, PER_GROUP)
                step(dve.scalar_tensor_tensor(in_group[:], local[0][:], -3.0e38, in_group[:], ALU.mult, ALU.add))
                first_best(local[1], in_group, PER_GROUP)
                for k in range(TOP_K):
                    step(dve.tensor_tensor(scratch[:], group_score[:], local[k][:], ALU.mult))
                    step(dve.tensor_reduce(weight[k][:], scratch[:], AX.X, ALU.add))
                    step(dve.tensor_tensor(
                        chosen[k][:].rearrange("p t (g k) -> p t g k", k=PER_GROUP), mask4,
                        local[k][:].unsqueeze(2).to_broadcast(by_group), ALU.mult))
                step(dve.tensor_tensor(either[:], chosen[0][:], chosen[1][:], ALU.add))
                dve.sem_inc(chosen_ready, 1)
                step(dve.tensor_tensor(best[:], weight[0][:], weight[1][:], ALU.add))
                step(dve.reciprocal(best[:], best[:]))
                for k in range(TOP_K):
                    step(dve.tensor_tensor(weight[k][:], weight[k][:], best[:], ALU.mult))
                step(dve.memset(before[:, 0, :], 0.0))
                dve.wait_ge(counted, 1)
                for t in range(TILES):
                    step(dve.tensor_tensor(before[:, t + 1, :], count_ps[:, t, :], before[:, t, :], ALU.add))
                shape = [P, EXPERTS, TILES]
                step(dve.tensor_tensor(over[:], before[:, TILES, :].unsqueeze(2).to_broadcast(shape),
                                       steps[:].unsqueeze(1).to_broadcast(shape), ALU.is_gt))
                step(dve.tensor_reduce(n_blocks[:], over[:], AX.X, ALU.add))
                step(dve.tensor_scalar(n_blocks[:], n_blocks[:], 1.0, None, ALU.max))
                step(dve.tensor_tensor_scan(ends[:], ones[:, 0:EXPERTS], n_blocks[:], 0.0, ALU.mult, ALU.add))
                step(dve.tensor_scalar(idle_blocks[:], ends[0:1, EXPERTS - 1:EXPERTS], -1.0, float(SLOT_BLOCKS),
                                       ALU.mult, ALU.add))
                step(dve.tensor_tensor(ends[:], ends[:], n_blocks[:], ALU.subtract))
                step(dve.tensor_copy(blocks_of[:], n_blocks[0:1, :]))
                step(dve.tensor_copy(first_block[:], ends[0:1, :]))
                step(dve.tensor_scalar(ends[:], ends[:], float(P), None, ALU.mult))
                step(dve.tensor_tensor(rank[:], rank_ps[:], before[:, 0:TILES, :], ALU.add))
                step(dve.tensor_tensor(rank[:], rank[:], ends[:].unsqueeze(1).to_broadcast(by_expert), ALU.add))
                for k in range(TOP_K):
                    step(dve.tensor_tensor(product[:], rank[:], chosen[k][:], ALU.mult))
                    step(dve.tensor_reduce(position[k][:], product[:], AX.X, ALU.add))
                    step(dve.tensor_copy(position_id[k][:], position[k][:]))
                    step(dve.tensor_scalar(table_id[k][:], position_id[k][:], P - 1, SLOT_BLOCKS.bit_length() - 1,
                                           ALU.bitwise_and, ALU.logical_shift_left))
                    step(dve.tensor_scalar(block_id[:], position_id[k][:], P.bit_length() - 1, None,
                                           ALU.logical_shift_right))
                    step(dve.tensor_tensor(table_id[k][:], table_id[k][:], block_id[:], ALU.bitwise_or))
                dve.sem_inc(routed, 1)


def experts(nc, const, first_block, blocks_of, idle_blocks, w_gate, w_up, w_down, h1_dram, slot_dram, y_dram):
    ident = const["ident"]
    with ExitStack() as ctx:
        m = Memory(nc, ctx)
        wg = [m.sb(f"e_wg{i}", [P, KC, D_EXPERT]) for i in range(2)]
        wu = [m.sb(f"e_wu{i}", [P, KC, D_EXPERT]) for i in range(2)]
        wd = [m.sb(f"e_wd{i}", [P, FC, D]) for i in range(2)]
        slots = m.sb("e_slots", [P, SLOT_BLOCKS], I32)
        block_slots = m.sb("e_block_slots", [P, 1], I32)
        tokens = m.sb("e_tokens", [P, D])
        tokens_tr = m.sb("e_tokens_tr", [P, KC, P])
        gated = m.sb("e_gated", [P, D_EXPERT])
        hidden = m.sb("e_hidden", [P, D_EXPERT])
        hidden_tr = m.sb("e_hidden_tr", [P, FC, P])
        result = m.sb("e_result", [P, D])
        zero = m.sb("e_zero", [P, D])
        tok_ps = m.ps("e_tok_ps", [P, KC, P])
        gate_ps, up_ps = m.ps("e_gate_ps", [P, D_EXPERT]), m.ps("e_up_ps", [P, D_EXPERT])
        hid_ps = m.ps("e_hid_ps", [P, FC, P])
        out_ps = m.ps("e_out_ps", [P, D])

        w_landed = [m.sem(f"e_w_landed{i}") for i in range(2)]
        expert_done = m.sem("e_expert_done")
        slots_landed, picked, gathered = m.sem("e_slots_landed"), m.sem("e_picked"), m.sem("e_gathered")
        tok_turned, tok_ready = m.sem("e_tok_turned"), m.sem("e_tok_ready")
        gate_made, up_made = m.sem("e_gate_made"), m.sem("e_up_made")
        gated_ready, hidden_ready = m.sem("e_gated_ready"), m.sem("e_hidden_ready")
        hid_turned, hid_ready = m.sem("e_hid_turned"), m.sem("e_hid_ready")
        passed = [m.sem(f"e_passed{i}") for i in range(4)]
        cleared, zero_ready = m.sem("e_cleared"), m.sem("e_zero_ready")
        down_made, result_ready, result_sent = m.sem("e_down_made"), m.sem("e_result_ready"), m.sem("e_result_sent")

        def each_expert(engine, step):
            with engine.Fori(0, EXPERTS // 2) as i:
                for b in range(2):
                    step(2 * i + b, b, i)

        def each_block(engine, body, around=lambda engine, expert, b, use, which: None):
            def step(expert, b, use):
                start = engine.value_load(first_block[0:1, bass.ds(expert, 1)], min_val=0, max_val=SLOT_BLOCKS - 1)
                count = engine.value_load(blocks_of[0:1, bass.ds(expert, 1)], min_val=1, max_val=TILES)
                around(engine, expert, b, use, "before")
                with engine.Fori(0, count) as k:
                    body(nc.s_assert_within(start + k, 0, SLOT_BLOCKS - 2, skip_runtime_bounds_check_because=
                                            "2 SEQ choices in blocks of 128 and a block for each idle expert "
                                            "are 63 blocks at most"), b)
                around(engine, expert, b, use, "after")
            each_expert(engine, step)

        with nc.Block() as block:

            @block.sync
            def _(sp):
                def load(expert, b, use):
                    at = sp.snap(expert)
                    sp.wait_ge(expert_done, expert + 1)
                    for dst, src in ((wg, w_gate), (wu, w_up), (wd, w_down)):
                        sp.dma_start(dst[b][:], src[bass.ds(at, 1), :, :].rearrange("e (k p) n -> p (e k) n", p=P)
                                     ).then_inc(w_landed[b], 16)

                idle = sp.value_load(idle_blocks[0:1, 0:1], min_val=1, max_val=SLOT_BLOCKS - EXPERTS)
                sp.wait_ge(zero_ready, 1)
                with sp.Fori(0, idle) as k:
                    sp.dma_start(y_dram[bass.ds(sp.snap((SLOT_BLOCKS - 1 - k) * P), P), :], zero[:]).then_inc(cleared, 16)

                each_expert(sp, load)
                sp.wait_ge(cleared, 16 * idle)
                sp.sem_inc(passed[3], 1)

            @block.gpsimd
            def _(pool):
                pool.dma_start(slots[:], slot_dram.rearrange("(p b) o -> p (b o)", b=SLOT_BLOCKS)
                               ).then_inc(slots_landed, 16)
                pool.wait_ge(slots_landed, 16)

                def gather(block):
                    pool.tensor_copy(block_slots[:], slots[:, bass.ds(block, 1)]).then_inc(picked, 1)
                    pool.wait_ge(picked, block + 1)
                    pool.sem_inc(passed[0], 1)
                    pool.indirect_dma_start(out=tokens[:], out_offset=None, in_=h1_dram,
                                            in_offset=bass.IndirectOffsetOnAxis(ap=block_slots[:, 0:1], axis=0)
                                            ).then_inc(gathered, 16)

                gather(0)

                def body(block, b):
                    pool.wait_ge(tok_turned, block + 1)
                    gather(block + 1)

                each_block(pool, body)

            @block.scalar
            def _(act):
                act.sem_inc(result_sent, 16)

                def copy_tokens(block):
                    act.wait_ge(tok_turned, block + 1)
                    act.wait_ge(up_made, block + 1)
                    act.copy(tokens_tr[:], tok_ps[:]).then_inc(tok_ready, 1)

                copy_tokens(0)

                def body(block, b):
                    act.wait_ge(gate_made, block + 1)
                    act.wait_ge(hidden_ready, block + 1)
                    act.activation(gated[:], gate_ps[:], ACT.Silu).then_inc(gated_ready, 1)
                    act.wait_ge(hid_turned, block + 1)
                    act.wait_ge(down_made, block + 1)
                    act.copy(hidden_tr[:], hid_ps[:]).then_inc(hid_ready, 1)
                    copy_tokens(block + 1)
                    row = act.snap(block * P)
                    act.wait_ge(result_ready, block + 2)
                    act.dma_start(y_dram[bass.ds(row, P), :], result[:]).then_inc(result_sent, 16)

                each_block(act, body)
                blocks = (act.value_load(first_block[0:1, EXPERTS - 1:EXPERTS], min_val=0, max_val=SLOT_BLOCKS - 1)
                          + act.value_load(blocks_of[0:1, EXPERTS - 1:EXPERTS], min_val=1, max_val=TILES))
                act.wait_ge(result_sent, 16 * blocks + 16)
                act.sem_inc(passed[2], 1)

            @block.vector
            def _(dve):
                dve.memset(zero[:], 0.0).then_inc(zero_ready, 1)
                dve.sem_inc(hidden_ready, 1)
                dve.sem_inc(result_ready, 1)

                def body(block, b):
                    dve.wait_ge(gated_ready, block + 1)
                    dve.wait_ge(up_made, block + 2)
                    dve.tensor_tensor(hidden[:], up_ps[:], gated[:], ALU.mult).then_inc(hidden_ready, 1)
                    dve.wait_ge(down_made, block + 2)
                    dve.wait_ge(result_sent, 16 * block + 16)
                    dve.tensor_copy(result[:], out_ps[:]).then_inc(result_ready, 1)

                each_block(dve, body)

            @block.tensor
            def _(pe):
                pe.sem_inc(expert_done, 2)
                pe.sem_inc(up_made, 1)
                pe.sem_inc(down_made, 1)

                def turn_tokens(block):
                    pe.wait_ge(gathered, 16 * block + 16)
                    for k in range(KC):
                        mm = pe.transpose(tok_ps[:, k, :], tokens[:, k * P:(k + 1) * P], ident[:])
                    mm.then_inc(tok_turned, 1)

                turn_tokens(0)

                def body(block, b):
                    pe.wait_ge(tok_ready, block + 1)
                    for k in range(KC):
                        mm = pe.matmul(gate_ps[:], tokens_tr[:, k, :], wg[b][:, k, :], start=k == 0, stop=k == KC - 1)
                    mm.then_inc(gate_made, 1)
                    for k in range(KC):
                        mm = pe.matmul(up_ps[:], tokens_tr[:, k, :], wu[b][:, k, :], start=k == 0, stop=k == KC - 1)
                    mm.then_inc(up_made, 1)
                    turn_tokens(block + 1)
                    pe.wait_ge(hidden_ready, block + 2)
                    for f in range(FC):
                        mm = pe.transpose(hid_ps[:, f, :], hidden[:, f * P:(f + 1) * P], ident[:])
                    mm.then_inc(hid_turned, 1)
                    pe.wait_ge(hid_ready, block + 1)
                    pe.wait_ge(result_ready, block + 1)
                    for half in range(2):
                        for f in range(FC):
                            mm = pe.matmul(out_ps[:, half * BANK:(half + 1) * BANK], hidden_tr[:, f, :],
                                           wd[b][:, f, half * BANK:(half + 1) * BANK], start=f == 0, stop=f == FC - 1)
                    mm.then_inc(down_made, 1)

                def around(engine, expert, b, use, which):
                    if which == "before":
                        engine.wait_ge(w_landed[b], 48 * use + 48)
                        engine.sem_inc(passed[1], 1)
                    else:
                        engine.drain().then_inc(expert_done, 1)

                each_block(pe, body, around)


def combine(nc, weight, position_id, ln_g, ln_b, h1_dram, y_dram, out):
    with ExitStack() as ctx:
        m = Memory(nc, ctx)
        gain, shift = m.sb("c_gain", [P, D]), m.sb("c_shift", [P, D])
        eps = m.sb("c_eps", [P, 1])
        rows = [m.sb(f"c_rows{i}", [P, D]) for i in range(2)]
        picked_id = [[m.sb(f"c_picked_id{i}_{k}", [P, 1], I32) for k in range(TOP_K)] for i in range(2)]
        y = [[m.sb(f"c_y{i}_{k}", [P, D]) for k in range(TOP_K)] for i in range(2)]
        stats, moments = m.sb("c_stats", [P, 2, 6]), m.sb("c_moments", [P, 2])
        rstd, offset = m.sb("c_rstd", [P, 1]), m.sb("c_offset", [P, 1])

        params_landed = m.sem("c_params_landed")
        const_ready = m.sem("c_const_ready")
        h_landed = [m.sem(f"c_h_landed{i}") for i in range(2)]
        y_landed = [m.sem(f"c_y_landed{i}") for i in range(2)]
        out_sent = [m.sem(f"c_out_sent{i}") for i in range(2)]
        picked, passed = m.sem("c_picked"), m.sem("c_passed")
        res_scaled, y_added = m.sem("c_res_scaled"), m.sem("c_y_added")
        half_stats, stats_seen, moments_ready = m.sem("c_half_stats"), m.sem("c_stats_seen"), m.sem("c_moments_ready")
        std_ready, rstd_ready, offset_ready = m.sem("c_std_ready"), m.sem("c_rstd_ready"), m.sem("c_offset_ready")
        scaled, gained, shifted = m.sem("c_scaled"), m.sem("c_gained"), m.sem("c_shifted")
        with nc.Block() as block:

            @block.sync
            def _(sp):
                for b in range(2):
                    sp.sem_inc(out_sent[b], 16)
                load_row(sp, gain[:], ln_g, params_landed)
                load_row(sp, shift[:], ln_b, params_landed)

                def at(t):
                    return t * P if isinstance(t, int) else sp.snap(t * P)

                def load(t, b, use):
                    tokens = at(t)
                    sp.wait_ge(out_sent[b], 16 * use + 16)
                    sp.dma_start(rows[b][:], h1_dram[bass.ds(tokens, P), :]).then_inc(h_landed[b], 16)

                def send(t, b, use):
                    tokens = at(t)
                    sp.wait_ge(shifted, t + 1)
                    sp.dma_start(out[bass.ds(tokens, P), :], rows[b][:]).then_inc(out_sent[b], 16)

                skewed(sp, (2, send), (0, load))
                for b in range(2):
                    sp.wait_ge(out_sent[b], 16 * (TILES // 2 + 1))

            @block.gpsimd
            def _(pool):
                pool.memset(eps[:], LN_EPS).then_inc(const_ready, 1)
                pool.wait_ge(params_landed, 32)

                def gather(t, b, use):
                    pool.wait_ge(y_added, TOP_K * t + TOP_K)
                    pool.sem_inc(picked, 1)
                    for k in range(TOP_K):
                        pool.tensor_copy(picked_id[b][k][:], position_id[k][:, bass.ds(t, 1)]).then_inc(picked, 1)
                    pool.wait_ge(picked, 3 * t + 3)
                    pool.sem_inc(passed, 1)
                    for k in range(TOP_K):
                        pool.indirect_dma_start(out=y[b][k][:], out_offset=None, in_=y_dram,
                                                in_offset=bass.IndirectOffsetOnAxis(ap=picked_id[b][k][:, 0:1], axis=0)
                                                ).then_inc(y_landed[b], 16)

                def add_shift(t, b, use):
                    pool.wait_ge(gained, t + 1)
                    pool.tensor_tensor(rows[b][:], rows[b][:], shift[:], ALU.add).then_inc(shifted, 1)

                skewed(pool, (0, gather), (1, add_shift))

            @block.scalar
            def _(act):
                act.preload_act_table_set("sqrt_and_others")
                act.wait_ge(const_ready, 1)

                def scale_residual(t, b, use):
                    act.wait_ge(h_landed[b], 16 * use + 16)
                    act.mul(rows[b][:], rows[b][:], ALPHA).then_inc(res_scaled, 1)

                def normalise(t, b, use):
                    act.wait_ge(moments_ready, t + 1)
                    act.activation(rstd[:], moments[:, 1:2], ACT.Sqrt, bias=eps[:]).then_inc(std_ready, 1)
                    act.wait_ge(offset_ready, t + 1)
                    act.activation(rows[b][:], rows[b][:], ACT.Identity, scale=rstd[:], bias=offset[:]
                                   ).then_inc(scaled, 1)

                skewed(act, (0, scale_residual), (1, normalise))

            @block.vector
            def _(dve):
                dve.sem_inc(y_added, 2 * TOP_K)
                dve.wait_ge(params_landed, 32)

                def add(t, b, use):
                    dve.wait_ge(res_scaled, t + 1)
                    dve.wait_ge(y_landed[b], 32 * use + 32)
                    for k in range(TOP_K):
                        dve.scalar_tensor_tensor(rows[b][:], y[b][k][:], weight[k][:, bass.ds(t, 1)], rows[b][:],
                                                 ALU.mult, ALU.add).then_inc(y_added, 1)
                        dve.wait_ge(y_added, 2 * TOP_K + TOP_K * t + k + 1)
                    for n in range(2):
                        dve.bn_stats(stats[:, n, :], rows[b][:, n * BANK:(n + 1) * BANK]).then_inc(half_stats, 1)
                    dve.wait_ge(half_stats, 2 * t + 2)
                    dve.sem_inc(stats_seen, 1)
                    dve.bn_aggr(moments[:], stats[:]).then_inc(moments_ready, 1)
                    dve.wait_ge(std_ready, t + 1)
                    dve.reciprocal(rstd[:], rstd[:]).then_inc(rstd_ready, 1)
                    dve.wait_ge(rstd_ready, t + 1)
                    dve.scalar_tensor_tensor(offset[:], moments[:, 0:1], -1.0, rstd[:], ALU.mult, ALU.mult
                                             ).then_inc(offset_ready, 1)
                    dve.wait_ge(scaled, t + 1)
                    dve.tensor_tensor(rows[b][:], rows[b][:], gain[:], ALU.mult).then_inc(gained, 1)

                skewed(dve, (1, add))


def decoder_layer(nc, x, ln0_g, ln0_b, w_in, conv_w, g_mix, w_out, ln_mix_g, ln_mix_b, router_w, router_b,
                  w_gate, w_up, w_down, ln_ffn_g, ln_ffn_b, out):
    def scratch(name, shape, dt=F32):
        return nc.dram_tensor(name, shape, dt, kind="Internal").ap()

    h_dram, h1_dram = scratch("h_scratch", (SEQ, D)), scratch("h1_scratch", (SEQ, D))
    qk_dram = scratch("qk_scratch", (2, 2 * D_ATTN, SEQ))
    v_dram = scratch("v_scratch", (HEADS, P, TILES, 2 * HEAD_DIM))
    mixed_dram = scratch("mixed_scratch", (D, SEQ))
    slot_dram = scratch("slot_scratch", (SLOTS, 1), I32)
    y_dram = scratch("y_scratch", (SLOTS, D))
    with ExitStack() as ctx:
        m = Memory(nc, ctx)
        const = {"ident": m.sb("ident", [P, P])}
        with ExitStack() as front:
            f = Memory(nc, front)
            h_tr = [f.sb(f"h_tr{i}", [P, KC, SEQ], F32R) for i in range(2)]
            norm_input(nc, const, h_tr, x, ln0_g, ln0_b, h_dram)
            project(nc, const, h_tr, w_in, conv_w, qk_dram, v_dram, mixed_dram)
        attend(nc, const, qk_dram, v_dram, mixed_dram)
        logits = m.sb("logits", [P, TILES, EXPERTS])
        weight = [m.sb(f"weight{k}", [P, TILES]) for k in range(TOP_K)]
        position_id = [m.sb(f"position_id{k}", [P, TILES], I32) for k in range(TOP_K)]
        first_block, blocks_of = m.sb("first_block", [1, EXPERTS], I32), m.sb("blocks_of", [1, EXPERTS], I32)
        idle_blocks = m.sb("idle_blocks", [1, 1], I32)
        mix(nc, const, logits, w_out, g_mix, ln_mix_g, ln_mix_b, router_w, h_dram, mixed_dram, h1_dram)
        route(nc, logits, weight, position_id, first_block, blocks_of, idle_blocks, router_b, slot_dram)
        experts(nc, const, first_block, blocks_of, idle_blocks, w_gate, w_up, w_down, h1_dram, slot_dram, y_dram)
        combine(nc, weight, position_id, ln_ffn_g, ln_ffn_b, h1_dram, y_dram, out)


def kernel(x, ln0_g, ln0_b, w_in, conv_w, g_conv, g_attn, w_out, ln_mix_g, ln_mix_b, router_w, router_b,
           w_gate, w_up, w_down, ln_ffn_g, ln_ffn_b):
    import numpy as np
    import concourse.bacc as bacc
    from concourse.bass_utils import run_bass_kernel_spmd

    def plain(a):
        return np.ascontiguousarray(a)

    arrays = {
        "x": plain(x).reshape(SEQ, D), "ln0_g": plain(ln0_g), "ln0_b": plain(ln0_b),
        "w_in": plain(w_in).reshape(D, 3 * D_CONV + 3 * D_ATTN),
        "conv_w": np.ascontiguousarray(plain(conv_w).reshape(CONV_K, CC, P).transpose(2, 0, 1)),
        "g_mix": np.ascontiguousarray(np.concatenate([plain(g_conv)[0], plain(g_attn)[0]]).reshape(KC, P).T),
        "w_out": plain(w_out).reshape(D, D), "ln_mix_g": plain(ln_mix_g).reshape(D),
        "ln_mix_b": plain(ln_mix_b).reshape(D), "router_w": plain(router_w), "router_b": plain(router_b),
        "w_gate": plain(w_gate).reshape(EXPERTS, D, D_EXPERT), "w_up": plain(w_up).reshape(EXPERTS, D, D_EXPERT),
        "w_down": plain(w_down).reshape(EXPERTS, D_EXPERT, D), "ln_ffn_g": plain(ln_ffn_g).reshape(D),
        "ln_ffn_b": plain(ln_ffn_b).reshape(D),
    }
    nc = bacc.Bacc("TRN2", target_bir_lowering=False, num_devices=1)
    args = [nc.dram_tensor(f"{name}_in", a.shape, F32, kind="ExternalInput").ap() for name, a in arrays.items()]
    out = nc.dram_tensor("out", (SEQ, D), F32, kind="ExternalOutput").ap()
    decoder_layer(nc, *args, out)
    r = run_bass_kernel_spmd(nc, [{f"{name}_in": a for name, a in arrays.items()}], core_ids=[0])
    return r.results[0]["out"].reshape(1, SEQ, D)
```

```python
from contextlib import ExitStack

import concourse.bass as bass
from concourse import mybir

F32 = mybir.dt.float32
F32R = mybir.dt.float32r
I32 = mybir.dt.int32
ALU = mybir.AluOpType
ACT = mybir.ActivationFunctionType
AX = mybir.AxisListType

P = 128
BANK = 512
SEQ, D = 2048, 1024
TILES = SEQ // P
KC = D // P
D_CONV = D // 2
D_ATTN = D - D_CONV
HEAD_DIM = 64
HEADS = D_ATTN // HEAD_DIM
CONV_K = 3
CC = D_CONV // P
TG = SEQ // BANK
EXPERTS, GROUPS, PER_GROUP, TOP_K = 32, 8, 4, 2
D_EXPERT = 512
FC = D_EXPERT // P
SLOT_BLOCKS = (SEQ * TOP_K + EXPERTS * P) // P
SLOTS = SLOT_BLOCKS * P
ALPHA = 2.0 ** 0.25
LN_EPS, RMS_EPS = 1e-5, 1e-6
SCALE = HEAD_DIM ** -0.5
MASKED = -2.0 ** 100
LOW_SPLIT = (1, 0, 1)
EXP_CAP = 2.0 ** 60


class Memory:

    def __init__(self, nc, ctx):
        self.nc, self.ctx, self.sems = nc, ctx, []
        ctx.callback(self.give_back)

    def sb(self, name, shape, dt=F32):
        return self.ctx.enter_context(self.nc.sbuf_tensor(name, shape, dt))

    def ps(self, name, shape, dt=F32):
        return self.ctx.enter_context(self.nc.psum_tensor(name, shape, dt))

    def sem(self, name):
        self.sems.append(self.nc.alloc_semaphore(name=name))
        return self.sems[-1]

    def give_back(self):
        if self.sems:
            self.nc.clear_and_free_semaphores(self.sems)
            self.nc.all_engine_barrier()


def skewed(engine, *stages, ring=2):
    deepest = -(-max(lag for lag, _ in stages) // ring) * ring

    def plain(slot):
        for lag, step in stages:
            if 0 <= slot - lag < TILES:
                step(slot - lag, (slot - lag) % ring, (slot - lag) // ring)

    for slot in range(deepest):
        plain(slot)
    with engine.Fori(0, (TILES - deepest) // ring) as i:
        for inner in range(ring):
            for lag, step in stages:
                ahead = deepest + inner - lag
                step(ring * i + ahead, ahead % ring, i + ahead // ring)
    for slot in range(TILES, TILES + deepest):
        plain(slot)


def load_row(engine, tile, vector, sem):
    engine.dma_start(tile, vector.partition_broadcast(P)).then_inc(sem, 16)


def norm_input(nc, const, h_tr, x, ln_g, ln_b, h_dram):
    ident = const["ident"]
    h_tr_hi, h_tr_lo = h_tr
    with ExitStack() as ctx:
        m = Memory(nc, ctx)
        rows = m.sb("n_rows", [P, TILES, D])
        gain, shift = m.sb("n_gain", [P, D]), m.sb("n_shift", [P, D])
        stats = m.sb("n_stats", [P, 2, 6])
        moments = m.sb("n_moments", [P, TILES, 2])
        rstd = m.sb("n_rstd", [P, TILES])
        offset = m.sb("n_offset", [P, TILES])
        eps = m.sb("n_eps", [P, 1])
        tr_ps = [m.ps(f"n_tr_ps{i}", [P, KC, P]) for i in range(2)]
        x_in = [m.sem(f"n_x_in{i}") for i in range(4)]
        params_in = m.sem("n_params_in")
        half_stats = m.sem("n_half_stats")
        moments_ready = m.sem("n_moments_ready")
        eps_ready = m.sem("n_eps_ready")
        std_ready = m.sem("n_std_ready")
        rstd_ready = m.sem("n_rstd_ready")
        offset_ready = m.sem("n_offset_ready")
        scaled = m.sem("n_scaled")
        gained = m.sem("n_gained")
        h_ready = m.sem("n_h_ready")
        transposed = m.sem("n_transposed")
        hi_ready = m.sem("n_hi_ready")
        tr_free = m.sem("n_tr_free")
        h_stored = m.sem("n_h_stored")
        id_zero = m.sem("n_id_zero")
        id_ready = m.sem("n_id_ready")
        passed = m.sem("n_passed")
        group = TILES // 4
        ahead = 3
        with nc.Block() as block:

            @block.sync
            def _(sp):
                for q in range(4):
                    sp.dma_start(rows[:, q * group:(q + 1) * group, :],
                                 x[q * group * P:(q + 1) * group * P, :].rearrange("(t p) d -> p t d", p=P)
                                 ).then_inc(x_in[q], 16)
                    if q == 0:
                        load_row(sp, gain[:], ln_g, params_in)
                        load_row(sp, shift[:], ln_b, params_in)
                with sp.Fori(0, TILES) as t:
                    sp.wait_ge(h_ready, t + 1)
                    sp.dma_start(h_dram[bass.ts(t, P), :], rows[:, t, :]).then_inc(h_stored, 16)
                sp.wait_ge(h_stored, 16 * TILES)

            @block.gpsimd
            def _(pool):
                pool.memset(ident[:], 0.0).then_inc(id_zero, 1)
                pool.wait_ge(id_zero, 1)
                pool.affine_select(out=ident[:], in_=ident[:], compare_op=ALU.not_equal, fill=1.0, base=0,
                                   pattern=[[-1, P]], channel_multiplier=1).then_inc(id_ready, 1)
                pool.wait_ge(params_in, 32)
                with pool.Fori(0, TILES) as t:
                    pool.wait_ge(gained, t + 1)
                    pool.tensor_tensor(rows[:, t, :], rows[:, t, :], shift[:], ALU.add).then_inc(h_ready, 1)

            @block.vector
            def _(dve):
                dve.memset(eps[:], LN_EPS).then_inc(eps_ready, 1)

                def moments_of(q):
                    quarter = slice(q * group, (q + 1) * group)
                    dve.wait_ge(x_in[q], 16)
                    for t in range(q * group, (q + 1) * group):
                        if t:
                            dve.wait_ge(moments_ready, t)
                        for half in range(2):
                            dve.bn_stats(stats[:, half, :], rows[:, t, half * BANK:(half + 1) * BANK]
                                         ).then_inc(half_stats, 1)
                        dve.wait_ge(half_stats, 2 * t + 2)
                        dve.bn_aggr(moments[:, t, :], stats[:]).then_inc(moments_ready, 1)
                    dve.wait_ge(std_ready, q + 1)
                    dve.reciprocal(rstd[:, quarter], rstd[:, quarter]).then_inc(rstd_ready, 1)
                    dve.wait_ge(rstd_ready, q + 1)
                    dve.scalar_tensor_tensor(offset[:, quarter], moments[:, quarter, 0], -1.0, rstd[:, quarter],
                                             ALU.mult, ALU.mult).then_inc(offset_ready, 1)

                def gain_rows(t):
                    dve.wait_ge(scaled, t + 1)
                    dve.tensor_tensor(rows[:, t, :], rows[:, t, :], gain[:], ALU.mult).then_inc(gained, 1)

                def low_part(t, parity):
                    dve.wait_ge(hi_ready, t + 1)
                    dve.tensor_tensor(h_tr_lo[:, :, bass.ts(t, P)], tr_ps[parity][:],
                                      h_tr_hi[:, :, bass.ts(t, P)].bitcast(F32), ALU.subtract).then_inc(tr_free, 1)

                moments_of(0)
                dve.wait_ge(params_in, 32)
                for t in range(ahead):
                    gain_rows(t)
                for q in range(3):
                    moments_of(q + 1)
                    with dve.Fori(0, group // 2) as i:
                        for parity in range(2):
                            gain_rows(q * group + 2 * i + parity + ahead)
                            low_part(q * group + 2 * i + parity, parity)
                for t in range(TILES - group, TILES):
                    if t + ahead < TILES:
                        gain_rows(t + ahead)
                    low_part(t, t % 2)

            @block.scalar
            def _(act):
                act.wait_ge(eps_ready, 1)

                def deviation(q):
                    quarter = slice(q * group, (q + 1) * group)
                    act.wait_ge(moments_ready, (q + 1) * group)
                    act.activation(rstd[:, quarter], moments[:, quarter, 1], ACT.Sqrt, bias=eps[:]
                                   ).then_inc(std_ready, 1)
                    act.wait_ge(offset_ready, q + 1)
                    act.sem_inc(passed, 1)

                def normalise(t):
                    act.activation(rows[:, t, :], rows[:, t, :], ACT.Identity, scale=rstd[:, bass.ds(t, 1)],
                                   bias=offset[:, bass.ds(t, 1)]).then_inc(scaled, 1)

                def high_part(t, parity):
                    act.wait_ge(transposed, t + 1)
                    act.copy(h_tr_hi[:, :, bass.ts(t, P)], tr_ps[parity][:]).then_inc(hi_ready, 1)

                deviation(0)
                with act.Fori(0, group) as t:
                    normalise(t)
                for q in range(1, 4):
                    deviation(q)
                    with act.Fori(0, group // 2) as i:
                        for parity in range(2):
                            normalise(q * group + 2 * i + parity)
                            high_part((q - 1) * group + 2 * i + parity, parity)
                with act.Fori(0, group // 2) as i:
                    for parity in range(2):
                        high_part(3 * group + 2 * i + parity, parity)

            @block.tensor
            def _(pe):
                pe.sem_inc(tr_free, 2)
                pe.wait_ge(id_ready, 1)
                for t in range(TILES):
                    pe.wait_ge(h_ready, t + 1)
                    pe.wait_ge(tr_free, t + 1)
                    for k in range(KC):
                        last = pe.transpose(tr_ps[t % 2][:, k, :], rows[:, t, k * P:(k + 1) * P], ident[:])
                    last.then_inc(transposed, 1)


def project(nc, const, h_tr, w_in, conv_w, qk_dram, v_dram, mixed_dram):
    ident = const["ident"]
    h_tr_hi, h_tr_lo = h_tr
    attn_cols = 3 * D_CONV
    v_first, conv_first = 8, 12
    n_chunks = 3 * D_ATTN // P + 3 * CC
    ahead = 2 * TG

    with ExitStack() as ctx:
        m = Memory(nc, ctx)
        w_raw = [m.sb(f"p_w_raw{i}", [P, KC, P]) for i in range(2)]
        w_hi = [m.sb(f"p_w_hi{i}", [P, KC, P], F32R) for i in range(2)]
        w_lo = [m.sb(f"p_w_lo{i}", [P, KC, P], F32R) for i in range(2)]
        qk_out = [m.sb(f"p_qk_out{i}", [P, 2, BANK], F32R) for i in range(2)]
        v_tr = [m.sb(f"p_v_tr{i}", [P, BANK]) for i in range(2)]
        v_out = [m.sb(f"p_v_out{i}", [P, BANK // P, 2, 2, HEAD_DIM], F32R) for i in range(2)]
        gate_c = m.sb("p_gate_c", [P, SEQ])
        padded = m.sb("p_padded", [P, CONV_K - 1 + SEQ])
        conv = m.sb("p_conv", [P, SEQ])
        taps = m.sb("p_taps", [P, CONV_K, CC])
        conv_out = [m.sb(f"p_conv_out{i}", [P, BANK]) for i in range(2)]
        proj_ps = [m.ps(f"p_proj_ps{i}", [P, BANK]) for i in range(TG)]
        v_ps = [m.ps(f"p_v_ps{i}", [P, BANK // P, 2, HEAD_DIM]) for i in range(2)]

        w_landed = [m.sem(f"p_w_landed{i}") for i in range(2)]
        taps_landed = m.sem("p_taps_landed")
        w_hi_ready, w_lo_ready = m.sem("p_w_hi_ready"), m.sem("p_w_lo_ready")
        projected = m.sem("p_projected")
        taken = m.sem("p_taken")
        qk_hi_ready = m.sem("p_qk_hi_ready")
        qk_sent = [m.sem(f"p_qk_sent{i}") for i in range(2)]
        v_turned = m.sem("p_v_turned")
        v_hi_ready, v_lo_ready = m.sem("p_v_hi_ready"), m.sem("p_v_lo_ready")
        v_sent = [m.sem(f"p_v_sent{i}") for i in range(2)]
        pad_ready = m.sem("p_pad_ready")
        tap_done = m.sem("p_tap_done")
        conv_sent = [m.sem(f"p_conv_sent{i}") for i in range(2)]

        def walk(engine, attn, conv_piece):
            for kind, base in (("q", 0), ("k", 4), ("v", v_first)):
                with engine.Fori(0, 2) as i:
                    for parity in range(2):
                        attn(kind, base + 2 * i + parity, parity, base // 2 + i + 1)
            with engine.Fori(0, CC // 2) as i:
                for half in range(2):
                    for n, part in enumerate((1, 2, 0)):
                        local = 3 * half + n
                        conv_piece(2 * i + half, part, conv_first + 6 * i + local, local % 2,
                                   conv_first // 2 + 3 * i + local // 2 + 1)

        with nc.Block() as block:

            @block.gpsimd
            def _(pool):
                def load(col, chunk, parity):
                    pool.wait_ge(w_lo_ready, chunk + 1)
                    pool.dma_start(w_raw[parity][:], w_in[:, bass.ds(col, P)].rearrange("(k p) c -> p k c", p=P)
                                   ).then_inc(w_landed[parity], 16)

                walk(pool, lambda kind, chunk, parity, use: load(attn_cols + chunk * P, chunk, parity),
                     lambda piece, part, chunk, parity, use: load(part * D_CONV + piece * P, chunk, parity))
                load(attn_cols, n_chunks, 0)

            @block.scalar
            def _(act):
                def split(chunk, parity, use):
                    act.wait_ge(w_landed[parity], 16 * use)
                    act.wait_ge(projected, TG * chunk + TG)
                    act.copy(w_hi[parity][:], w_raw[parity][:]).then_inc(w_hi_ready, 1)

                def attn(kind, chunk, parity, use):
                    for tg in range(TG):
                        b = tg % 2
                        if tg == 1:
                            split(chunk + 1, 1 - parity, use + parity)
                        if kind == "v":
                            step = TG * (chunk - v_first) + tg
                            act.wait_ge(v_turned, step + 3)
                            act.wait_ge(v_sent[b], 32 * (2 * (chunk - v_first) + tg // 2 + 1))
                            act.copy(v_out[b][:, :, :, 0, :], v_ps[b][:]).then_inc(v_hi_ready, 1)
                        else:
                            act.wait_ge(projected, ahead + TG * chunk + tg + 1)
                            act.wait_ge(qk_sent[b], 16 * (2 * chunk + tg // 2 + 1))
                            act.activation(qk_out[b][:, 0, :], proj_ps[tg][:], ACT.Copy,
                                           scale=SCALE if kind == "q" else 1.0).then_inc(qk_hi_ready, 1)

                split(0, 0, 1)
                walk(act, attn, lambda piece, part, chunk, parity, use: split(chunk + 1, 1 - parity, use + parity))

            @block.vector
            def _(dve):
                dve.sem_inc(w_lo_ready, 2)
                dve.sem_inc(taken, TG)
                dve.sem_inc(v_lo_ready, 2)
                dve.sem_inc(tap_done, CONV_K)
                dve.memset(padded[:, 0:CONV_K - 1], 0.0).then_inc(pad_ready, 1)

                def split(chunk, parity):
                    dve.wait_ge(w_hi_ready, chunk + 1)
                    dve.tensor_tensor(w_lo[parity][:], w_raw[parity][:], w_hi[parity][:].bitcast(F32), ALU.subtract
                                      ).then_inc(w_lo_ready, 1)

                def attn(kind, chunk, parity, use):
                    def v_low(tg):
                        b, step = tg % 2, TG * (chunk - v_first) + tg
                        dve.wait_ge(v_hi_ready, step + 1)
                        dve.tensor_tensor(v_out[b][:, :, :, 1, :], v_ps[b][:], v_out[b][:, :, :, 0, :].bitcast(F32),
                                          ALU.subtract).then_inc(v_lo_ready, 1)

                    for tg in range(TG):
                        b = tg % 2
                        if tg == 2:
                            split(chunk + 1, 1 - parity)
                        if kind == "v":
                            dve.wait_ge(projected, ahead + TG * chunk + tg + 1)
                            dve.wait_ge(v_turned, TG * (chunk - v_first) + tg + 1)
                            dve.tensor_copy(v_tr[b][:], proj_ps[tg][:]).then_inc(taken, 1)
                            if tg:
                                v_low(tg - 1)
                        else:
                            dve.wait_ge(qk_hi_ready, TG * chunk + tg + 1)
                            dve.scalar_tensor_tensor(qk_out[b][:, 1, :], proj_ps[tg][:], SCALE if kind == "q" else 1.0,
                                                     qk_out[b][:, 0, :].bitcast(F32), ALU.mult, ALU.subtract
                                                     ).then_inc(taken, 1)
                    if kind == "v":
                        v_low(TG - 1)

                def conv_piece(piece, part, chunk, parity, use):
                    for tg in range(TG):
                        b, cols = tg % 2, slice(tg * BANK, (tg + 1) * BANK)
                        if tg == 2:
                            split(chunk + 1, 1 - parity)
                        dve.wait_ge(projected, ahead + TG * chunk + tg + 1)
                        if part == 1:
                            dve.wait_ge(taken, TG * chunk + tg + 1)
                            dve.tensor_copy(gate_c[:, cols], proj_ps[tg][:]).then_inc(taken, 1)
                        elif part == 2:
                            dve.wait_ge(taken, TG * (chunk - 1) + TG + tg + 1)
                            if tg == 0:
                                dve.wait_ge(tap_done, CONV_K * (piece + 1))
                            dve.tensor_tensor(padded[:, CONV_K - 1 + tg * BANK:CONV_K - 1 + (tg + 1) * BANK],
                                              proj_ps[tg][:], gate_c[:, cols], ALU.mult).then_inc(taken, 1)
                        else:
                            dve.wait_ge(conv_sent[b], 16 * (2 * piece + tg // 2 + 1))
                            dve.tensor_tensor(conv_out[b][:], proj_ps[tg][:], conv[:, cols], ALU.mult
                                              ).then_inc(taken, 1)
                    if part == 2:
                        dve.wait_ge(taken, TG * (chunk + 2))
                        for n in range(CONV_K):
                            tap = CONV_K - 1 - n
                            if n == 0:
                                dve.tensor_scalar(conv[:], padded[:, tap:tap + SEQ], taps[:, tap, bass.ds(piece, 1)],
                                                  None, ALU.mult).then_inc(tap_done, 1)
                            else:
                                dve.wait_ge(tap_done, CONV_K * (piece + 1) + n)
                                dve.scalar_tensor_tensor(conv[:], padded[:, tap:tap + SEQ],
                                                         taps[:, tap, bass.ds(piece, 1)], conv[:], ALU.mult, ALU.add
                                                         ).then_inc(tap_done, 1)
                        dve.wait_ge(tap_done, CONV_K * (piece + 2))

                dve.wait_ge(taps_landed, 16)
                dve.wait_ge(pad_ready, 1)
                split(0, 0)
                walk(dve, attn, conv_piece)

            @block.sync
            def _(sp):
                sp.dma_start(taps[:], conv_w).then_inc(taps_landed, 16)
                for b in range(2):
                    sp.sem_inc(qk_sent[b], 16)
                    sp.sem_inc(v_sent[b], 32)
                    sp.sem_inc(conv_sent[b], 16)

                def attn(kind, chunk, parity, use):
                    row = sp.snap((chunk - v_first) * 2 if kind == "v" else chunk * P)
                    for tg in range(TG):
                        b, tokens = tg % 2, slice(tg * BANK, (tg + 1) * BANK)
                        if kind == "v":
                            sp.wait_ge(v_lo_ready, TG * (chunk - v_first) + tg + 3)
                            for head in range(2):
                                sp.dma_start(
                                    v_dram[bass.ds(row + head, 1), :, tg * (BANK // P):(tg + 1) * (BANK // P), :
                                           ].rearrange("h p t d -> p (h t) d"),
                                    v_out[b][:, :, head, :, :].rearrange("p t s d -> p t (s d)").bitcast(F32)).then_inc(v_sent[b], 16)
                        else:
                            sp.wait_ge(taken, TG * chunk + tg + 1 + TG)
                            sp.dma_start(qk_dram[:, bass.ds(row, P), tokens].rearrange("s c t -> c s t"),
                                           qk_out[b][:].bitcast(F32)).then_inc(qk_sent[b], 16)

                def conv_piece(piece, part, chunk, parity, use):
                    if part == 0:
                        row = sp.snap(piece * P)
                        for tg in range(TG):
                            b = tg % 2
                            sp.wait_ge(taken, TG * chunk + tg + 1 + TG)
                            sp.dma_start(mixed_dram[bass.ds(row, P), tg * BANK:(tg + 1) * BANK],
                                           conv_out[b][:]).then_inc(conv_sent[b], 16)

                walk(sp, attn, conv_piece)
                for b in range(2):
                    sp.wait_ge(qk_sent[b], 16 * (2 * v_first + 1))
                    sp.wait_ge(v_sent[b], 32 * (2 * CC + 1))
                    sp.wait_ge(conv_sent[b], 16 * (2 * CC + 1))

            @block.tensor
            def _(pe):
                pe.sem_inc(projected, ahead)
                pe.sem_inc(v_turned, 2)

                def product(chunk, parity, tg):
                    pe.wait_ge(taken, TG * chunk + tg + 1)
                    terms = [(k, w, h) for k in range(KC) for w, h in
                             ((w_hi, h_tr_hi), (w_hi, h_tr_lo), (w_lo, h_tr_hi))]
                    for n, (k, w, h) in enumerate(terms):
                        last = pe.matmul(proj_ps[tg][:], w[parity][:, k, :], h[:, k, tg * BANK:(tg + 1) * BANK],
                                         start=n == 0, stop=n == len(terms) - 1)
                    last.then_inc(projected, 1)

                def turn_v(chunk, tg):
                    b, step = tg % 2, TG * (chunk - v_first) + tg
                    pe.wait_ge(taken, TG * chunk + tg + 1 + TG)
                    pe.wait_ge(v_lo_ready, step + 1)
                    for n in range(BANK // P):
                        last = pe.transpose(v_ps[b][:, n, :, :].rearrange("p h d -> p (h d)"),
                                            v_tr[b][:, n * P:(n + 1) * P], ident[:])
                    last.then_inc(v_turned, 1)

                def attn(kind, chunk, parity, use):
                    pe.wait_ge(w_lo_ready, chunk + 3)
                    for tg in range(TG):
                        product(chunk, parity, tg)
                        if kind == "v" and tg:
                            turn_v(chunk, tg - 1)
                    if kind == "v":
                        turn_v(chunk, TG - 1)

                def conv_piece(piece, part, chunk, parity, use):
                    pe.wait_ge(w_lo_ready, chunk + 3)
                    for tg in range(TG):
                        product(chunk, parity, tg)

                walk(pe, attn, conv_piece)


def attend(nc, const, w_raw, w_landed, w_out, qk_dram, v_dram, mixed_dram):
    queries = BANK
    per_group = queries // P
    steps = []
    for head in range(2):
        for group in range(TG):
            for j in range(per_group * group + per_group - 1, -1, -1):
                steps.append((head, group, j, max(0, j - per_group * group) * P))
    n_steps = len(steps)
    first = [j == per_group * group + per_group - 1 for _, group, j, _ in steps]
    last = [j == 0 for _, _, j, _ in steps]
    diagonal = [j >= per_group * group for _, group, j, _ in steps]
    adds = [0]
    for n in range(n_steps):
        adds.append(adds[-1] + (not last[n]))
    clears = [0]
    for n in range(n_steps):
        clears.append(clears[-1] + (steps[n][3] > 0))
    groups_before = [0]
    for n in range(n_steps):
        groups_before.append(groups_before[-1] + last[n])
    maker = [LOW_SPLIT[n % len(LOW_SPLIT)] for n in range(n_steps)]
    made = [[0, 0]]
    for n in range(n_steps):
        made.append([made[-1][e] + (maker[n] == e) for e in range(2)])
    Z, E_BUFS, S_BUFS, T_BUFS, W_BUFS = 6, 4, 5, 5, 6
    SUFFIX_LAG, VALUE_LAG = 3, 8
    LN_LAG, ADD_LAG, EXP_LAG, EVAC_LAG = 1, 1, 4, 9

    def wait_low(engine, r, n):
        for e in (0, 1) if n < 0 else (maker[n],):
            engine.wait_ge(wts_lo_ready[e], made[-1][e] * r + made[max(n + 1, 0)][e] + 1)

    def low_part(engine, e, r, n):
        lo, w = steps[n][3], n % W_BUFS
        engine.wait_ge(wts_hi_ready, n_steps * r + n + 1)
        engine.tensor_tensor(wts_lo[w][:, lo:], wts[w][:, lo:], wts_hi[w][:, lo:].bitcast(F32), ALU.subtract
                             ).then_inc(wts_lo_ready[e], 1)

    def free(n, size):
        return max(n + 1, size)

    with ExitStack() as ctx:
        m = Memory(nc, ctx)
        keys = [m.sb(f"a_keys{i}", [P, SEQ], F32R) for i in range(2)]
        q_hi = [m.sb(f"a_q_hi{i}", [P, SEQ], F32R) for i in range(2)]
        q_lo = [m.sb(f"a_q_lo{i}", [P, SEQ], F32R) for i in range(2)]
        vals = [m.sb(f"a_vals{i}", [P, TILES, P], F32R) for i in range(2)]
        expz = [m.sb(f"a_expz{i}", [P, BANK]) for i in range(E_BUFS)]
        keep = [m.sb(f"a_keep{i}", [P, BANK]) for i in range(S_BUFS)]
        keep_hi = [m.sb(f"a_keep_hi{i}", [P, BANK], F32R) for i in range(W_BUFS)]
        keep_lo = [m.sb(f"a_keep_lo{i}", [P, BANK], F32R) for i in range(W_BUFS)]
        total = [m.sb(f"a_total{i}", [P, BANK]) for i in range(T_BUFS)]
        wts = [m.sb(f"a_wts{i}", [P, BANK]) for i in range(W_BUFS)]
        wts_hi = [m.sb(f"a_wts_hi{i}", [P, BANK], F32R) for i in range(W_BUFS)]
        wts_lo = [m.sb(f"a_wts_lo{i}", [P, BANK], F32R) for i in range(W_BUFS)]
        tri_f = m.sb("a_tri_f", [P, P])
        tri = m.sb("a_tri", [P, P], F32R)
        square = m.sb("a_square", [P, P])
        hidden_f, hidden = m.sb("a_hidden_f", [P, P]), m.sb("a_hidden", [P, P], F32R)
        ident = m.sb("a_ident", [P, P], F32R)
        zero = m.sb("a_zero", [P, P])
        blank_f = m.sb("a_blank_f", [P, BANK])
        blank = m.sb("a_blank", [P, BANK], F32R)
        half_out = [m.sb(f"a_half_out{i}", [HEAD_DIM, BANK]) for i in range(2)]
        head_out = [m.sb(f"a_head_out{i}", [HEAD_DIM, BANK]) for i in range(2)]
        z_ps = [m.ps(f"a_z_ps{i}", [P, BANK]) for i in range(Z)]
        out_ps = [m.ps(f"a_out_ps{i}", [P, BANK]) for i in range(2)]

        head_landed = [m.sem(f"a_head_landed{i}") for i in range(2)]
        vals_landed = [m.sem(f"a_vals_landed{i}") for i in range(2)]
        const_ready = m.sem("a_const_ready")
        tri_ready = m.sem("a_tri_ready")
        z_ready = m.sem("a_z_ready")
        exp_ready, capped, ln_ready = m.sem("a_exp_ready"), m.sem("a_capped"), m.sem("a_ln_ready")
        keep_raw = m.sem("a_keep_raw")
        keep_hi_ready, keep_lo_ready = m.sem("a_keep_hi_ready"), m.sem("a_keep_lo_ready")
        total_cleared, total_ready = m.sem("a_total_cleared"), m.sem("a_total_ready")
        suffix_ready = m.sem("a_suffix_ready")
        wts_raw = m.sem("a_wts_raw")
        wts_hi_ready = m.sem("a_wts_hi_ready")
        wts_lo_ready = [m.sem(f"a_wts_lo_ready{e}") for e in range(2)]
        valued = m.sem("a_valued")
        half_ready, out_ready = m.sem("a_half_ready"), m.sem("a_out_ready")
        out_sent = [m.sem(f"a_out_sent{i}") for i in range(2)]
        rounds = HEADS // 2

        with nc.Block() as block:

            @block.sync
            def _(sp):
                for b in range(2):
                    sp.sem_inc(out_sent[b], 16)

                def stage_in(r, b):
                    head = sp.snap(2 * r + b) if not isinstance(r, int) else 2 * r + b
                    for part in range(2):
                        rows = slice(part * HEAD_DIM, (part + 1) * HEAD_DIM)
                        k_rows, q_rows = bass.ds(D_ATTN + head * HEAD_DIM, HEAD_DIM), bass.ds(head * HEAD_DIM, HEAD_DIM)
                        for dst, src in ((keys, qk_dram[part, k_rows, :]), (q_hi, qk_dram[0, q_rows, :]),
                                         (q_lo, qk_dram[1, q_rows, :])):
                            sp.dma_start(dst[b][rows, :].bitcast(F32), src).then_inc(head_landed[b], 16)
                    sp.dma_start(vals[b][:].bitcast(F32), v_dram[bass.ds(head, 1), :, :, :].rearrange(
                        "h p t d -> p (h t) d")).then_inc(vals_landed[b], 16)

                def send_head(r, b):
                    for group in range(TG):
                        n = TG * b + group
                        row = sp.snap(D_CONV + (2 * r + b) * HEAD_DIM)
                        sp.wait_ge(out_ready, 2 * TG * r + n + 2)
                        sp.dma_start(mixed_dram[bass.ds(row, HEAD_DIM), group * BANK:(group + 1) * BANK],
                                     head_out[n % 2][:]).then_inc(out_sent[n % 2], 16)

                stage_in(0, 0)
                stage_in(0, 1)
                sp.dma_start(w_raw[:], w_out.rearrange("(k p) n -> p k n", p=P)).then_inc(w_landed, 16)
                with sp.Fori(0, rounds - 1) as r:
                    for b in range(2):
                        send_head(r, b)
                        stage_in(r + 1, b)
                for b in range(2):
                    for group in range(TG):
                        n = TG * b + group
                        row = D_CONV + (2 * (rounds - 1) + b) * HEAD_DIM
                        sp.wait_ge(out_ready, 2 * TG * (rounds - 1) + n + 2)
                        sp.dma_start(mixed_dram[row:row + HEAD_DIM, group * BANK:(group + 1) * BANK],
                                     head_out[n % 2][:]).then_inc(out_sent[n % 2], 16)
                for b in range(2):
                    sp.wait_ge(out_sent[b], 16 * (TG * rounds + 1))

            @block.gpsimd
            def _(pool):
                pool.memset(square[:], -1.0).then_inc(const_ready, 1)
                pool.memset(tri_f[:], -1.0).then_inc(const_ready, 1)
                pool.memset(hidden_f[:], 0.0).then_inc(const_ready, 1)
                pool.memset(zero[:], 0.0).then_inc(const_ready, 1)
                pool.memset(blank_f[:], 0.0).then_inc(const_ready, 1)
                pool.wait_ge(const_ready, 5)
                pool.affine_select(out=tri_f[:], in_=tri_f[:], compare_op=ALU.is_ge, fill=0.0, base=0,
                                   pattern=[[-1, P]], channel_multiplier=1).then_inc(const_ready, 1)
                pool.affine_select(out=hidden_f[:], in_=hidden_f[:], compare_op=ALU.is_gt, fill=MASKED, base=0,
                                   pattern=[[1, P]], channel_multiplier=-1).then_inc(const_ready, 1)
                pool.sem_inc(total_ready, 1)
                pool.sem_inc(wts_lo_ready[1], 1)
                with pool.Fori(0, rounds) as r:
                    for slot in range(n_steps + EVAC_LAG):
                        n = slot - EXP_LAG - 1
                        if 0 <= n < n_steps and maker[n] == 1:
                            low_part(pool, 1, r, n)
                        n = slot - ADD_LAG
                        if 0 <= n < n_steps and not last[n]:
                            lo = steps[n][3]
                            dst, src = total[(n + 1) % T_BUFS], total[n % T_BUFS]
                            pool.wait_ge(suffix_ready, n_steps * r + max(n + 1 - T_BUFS + 2, 1))
                            if lo:
                                pool.tensor_tensor(dst[:, lo - P:lo], zero[:], zero[:], ALU.add
                                                   ).then_inc(total_cleared, 1)
                                pool.wait_ge(total_cleared, clears[-1] * r + clears[n] + 1)
                            pool.wait_ge(keep_raw, E_BUFS + n_steps * r + n + 1)
                            if first[n]:
                                pool.tensor_tensor(dst[:, lo:], keep[n % S_BUFS][:, lo:], zero[:], ALU.add
                                                   ).then_inc(total_ready, 1)
                            else:
                                pool.wait_ge(total_ready, adds[-1] * r + adds[n] + 1)
                                pool.tensor_tensor(dst[:, lo:], src[:, lo:], keep[n % S_BUFS][:, lo:], ALU.add
                                                   ).then_inc(total_ready, 1)

            @block.scalar
            def _(act):
                act.wait_ge(const_ready, 7)
                act.copy(tri[:], tri_f[:]).then_inc(tri_ready, 1)
                act.copy(blank[:], blank_f[:]).then_inc(tri_ready, 1)
                act.copy(hidden[:], hidden_f[:]).then_inc(tri_ready, 1)
                act.copy(ident[:], const["ident"][:]).then_inc(tri_ready, 1)
                with act.Fori(0, rounds) as r:
                    act.preload_act_table_set("natural_log_exp_and_others")
                    base = n_steps * r
                    for slot in range(n_steps + EVAC_LAG):
                        n = slot - EXP_LAG
                        if 0 <= n < n_steps:
                            lo = steps[n][3]
                            act.wait_ge(suffix_ready, base + n + 2)
                            wait_low(act, r, n - W_BUFS)
                            act.activation(wts[n % W_BUFS][:, lo:], z_ps[n % Z][:, lo:], ACT.Exp).then_inc(wts_raw, 1)
                        n = slot
                        if n < n_steps:
                            lo = steps[n][3]
                            act.wait_ge(z_ready, base + n + 1)
                            act.wait_ge(keep_raw, base + free(n, E_BUFS))
                            act.activation(expz[n % E_BUFS][:, lo:], z_ps[n % Z][:, lo:], ACT.Exp
                                           ).then_inc(exp_ready, 1)
                        n = slot - LN_LAG
                        if 0 <= n < n_steps:
                            lo = steps[n][3]
                            act.wait_ge(capped, base + n + 1)
                            act.activation(expz[n % E_BUFS][:, lo:], expz[n % E_BUFS][:, lo:], ACT.Ln, bias=1.0
                                           ).then_inc(ln_ready, 1)
                        n = slot - EXP_LAG - 1
                        if 0 <= n < n_steps:
                            lo = steps[n][3]
                            act.wait_ge(wts_raw, base + n + 1)
                            act.wait_ge(valued, base + free(n, W_BUFS))
                            act.copy(wts_hi[n % W_BUFS][:, lo:], wts[n % W_BUFS][:, lo:]).then_inc(wts_hi_ready, 1)
                        n = slot - EVAC_LAG
                        if 0 <= n < n_steps and last[n]:
                            g = groups_before[n]
                            act.wait_ge(valued, base + n + 1 + W_BUFS)
                            act.wait_ge(out_ready, 2 * TG * r + max(g, 1))
                            act.copy(half_out[g % 2][:], out_ps[g % 2][HEAD_DIM:, :]).then_inc(half_ready, 1)

            @block.vector
            def _(dve):
                dve.sem_inc(keep_raw, E_BUFS)
                dve.sem_inc(out_ready, 1)
                dve.sem_inc(wts_lo_ready[0], 1)
                with dve.Fori(0, rounds) as r:
                    base = n_steps * r
                    for slot in range(n_steps + EVAC_LAG):
                        n = slot - LN_LAG
                        if 0 <= n < n_steps:
                            lo, s = steps[n][3], keep[n % S_BUFS]
                            dve.wait_ge(ln_ready, base + n + 1)
                            dve.wait_ge(total_ready, adds[-1] * r + adds[max(n - S_BUFS + 1, 0)] + 1)
                            dve.tensor_tensor(s[:, lo:], z_ps[n % Z][:, lo:], expz[n % E_BUFS][:, lo:], ALU.max
                                              ).then_inc(keep_raw, 1)
                        n = slot
                        if n < n_steps:
                            lo = steps[n][3]
                            dve.wait_ge(exp_ready, base + n + 1)
                            dve.tensor_scalar(expz[n % E_BUFS][:, lo:], expz[n % E_BUFS][:, lo:], EXP_CAP, None,
                                              ALU.min).then_inc(capped, 1)
                        n = slot - LN_LAG
                        if 0 <= n < n_steps:
                            lo, s, w = steps[n][3], keep[n % S_BUFS], n % W_BUFS
                            dve.wait_ge(keep_raw, base + E_BUFS + n + 1)
                            dve.wait_ge(suffix_ready, base + max(n + 2 - W_BUFS, 1))
                            dve.tensor_copy(keep_hi[w][:, lo:], s[:, lo:]).then_inc(keep_hi_ready, 1)
                        n = slot - EXP_LAG - 1
                        if 0 <= n < n_steps and maker[n] == 0:
                            low_part(dve, 0, r, n)
                        n = slot - LN_LAG
                        if 0 <= n < n_steps:
                            lo, s, w = steps[n][3], keep[n % S_BUFS], n % W_BUFS
                            dve.wait_ge(keep_hi_ready, base + n + 1)
                            dve.tensor_tensor(keep_lo[w][:, lo:], s[:, lo:], keep_hi[w][:, lo:].bitcast(F32),
                                              ALU.subtract).then_inc(keep_lo_ready, 1)
                        n = slot - EVAC_LAG
                        if 0 <= n < n_steps and last[n]:
                            g = groups_before[n]
                            dve.wait_ge(half_ready, 2 * TG * r + g + 1)
                            dve.wait_ge(out_sent[g % 2], 16 * (TG * r + g // 2 + 1))
                            dve.tensor_tensor(head_out[g % 2][:], out_ps[g % 2][:HEAD_DIM, :], half_out[g % 2][:],
                                              ALU.add).then_inc(out_ready, 1)

            @block.tensor
            def _(pe):
                pe.sem_inc(suffix_ready, 1)
                pe.sem_inc(valued, W_BUFS)
                pe.wait_ge(tri_ready, 4)
                with pe.Fori(0, rounds) as r:
                    base = n_steps * r
                    for slot in range(n_steps + VALUE_LAG):
                        n = slot
                        if n < n_steps:
                            b, group, j, lo = steps[n]
                            cols = slice(group * BANK + lo, (group + 1) * BANK)
                            if j == per_group - 1 and group == 0:
                                pe.wait_ge(head_landed[b], 6 * 16 * (r + 1))
                            if n >= Z:
                                pe.wait_ge(wts_raw, base + n + 1 - Z)
                            for i, q in enumerate((q_hi, q_lo)):
                                mm = pe.matmul(z_ps[n % Z][:, lo:], keys[b][:, j * P:(j + 1) * P], q[b][:, cols],
                                               start=i == 0, stop=i == 1 and not diagonal[n])
                            if diagonal[n]:
                                mm = pe.matmul(z_ps[n % Z][:, lo:lo + P], ident[:], hidden[:], start=False, stop=True)
                            mm.then_inc(z_ready, 1)
                        n = slot - VALUE_LAG
                        if 0 <= n < n_steps:
                            b, group, j, lo = steps[n]
                            w, g = n % W_BUFS, groups_before[n]
                            if first[n]:
                                if group == 0:
                                    pe.wait_ge(vals_landed[b], 16 * (r + 1))
                                pe.wait_ge(out_ready, 2 * TG * r + max(g, 1))
                                pe.matmul(out_ps[g % 2][:], tri[:], blank[:], start=True, stop=False)
                            wait_low(pe, r, n)
                            pe.matmul(out_ps[g % 2][:, lo:], vals[b][:, j, :], wts_hi[w][:, lo:], start=False,
                                      stop=False)
                            pe.matmul(out_ps[g % 2][:, lo:], vals[b][:, j, :], wts_lo[w][:, lo:], start=False,
                                      stop=last[n]).then_inc(valued, 1)
                        n = slot - SUFFIX_LAG
                        if 0 <= n < n_steps:
                            lo, w = steps[n][3], n % W_BUFS
                            if not first[n]:
                                skip = P if diagonal[n] else 0
                                pe.wait_ge(total_ready, adds[-1] * r + adds[n] + 1)
                                pe.wait_ge(keep_raw, E_BUFS + base + n + 1)
                                pe.matmul(z_ps[n % Z][:, lo + skip:], square[:], total[n % T_BUFS][:, lo + skip:],
                                          start=False, stop=False, skip_group_check=True)
                            pe.wait_ge(keep_lo_ready, base + n + 1)
                            pe.matmul(z_ps[n % Z][:, lo:], tri[:], keep_hi[w][:, lo:], start=False, stop=False,
                                      skip_group_check=True)
                            pe.matmul(z_ps[n % Z][:, lo:], tri[:], keep_lo[w][:, lo:], start=False, stop=True,
                                      skip_group_check=True).then_inc(suffix_ready, 1)


def mix(nc, const, logits, w_raw, w_landed, g_mix, ln_g, ln_b, router_w, h_dram, mixed_dram, h1_dram):
    ident = const["ident"]
    with ExitStack() as ctx:
        m = Memory(nc, ctx)
        w_hi, w_lo = m.sb("m_w_hi", [P, KC, D], F32R), m.sb("m_w_lo", [P, KC, D], F32R)
        row_gain = m.sb("m_row_gain", [P, KC])
        gain, shift = m.sb("m_gain", [P, D]), m.sb("m_shift", [P, D])
        router = m.sb("m_router", [P, KC, EXPERTS])
        ones = m.sb("m_ones", [P, 1])
        eps = m.sb("m_eps", [P, 2])
        ch_raw = [m.sb(f"m_ch_raw{i}", [P, KC, P]) for i in range(2)]
        ch_hi = [m.sb(f"m_ch_hi{i}", [P, KC, P], F32R) for i in range(2)]
        ch_lo = [m.sb(f"m_ch_lo{i}", [P, KC, P], F32R) for i in range(2)]
        square = [m.sb(f"m_square{i}", [P, KC, P]) for i in range(2)]
        folded = [m.sb(f"m_folded{i}", [P, 2, P]) for i in range(2)]
        rows = [m.sb(f"m_rows{i}", [P, D]) for i in range(2)]
        h1_tr = m.sb("m_h1_tr", [P, KC, P])
        rms = m.sb("m_rms", [P, 2])
        stats, moments = m.sb("m_stats", [P, 2, 6]), m.sb("m_moments", [P, 2])
        rstd, offset = m.sb("m_rstd", [P, 1]), m.sb("m_offset", [P, 1])
        conv_ps, attn_ps = m.ps("m_conv_ps", [P, D]), m.ps("m_attn_ps", [P, D])
        tr_ps = m.ps("m_tr_ps", [P, KC, P])
        rms_ps = m.ps("m_rms_ps", [P, BANK])
        logit_ps = m.ps("m_logit_ps", [P, BANK])

        row_gain_landed, params_landed = m.sem("m_row_gain_landed"), m.sem("m_params_landed")
        w_gained, w_hi_ready, w_lo_ready = m.sem("m_w_gained"), m.sem("m_w_hi_ready"), m.sem("m_w_lo_ready")
        const_ready = m.sem("m_const_ready")
        ch_landed = [m.sem(f"m_ch_landed{i}") for i in range(2)]
        h_landed = [m.sem(f"m_h_landed{i}") for i in range(2)]
        h1_sent = [m.sem(f"m_h1_sent{i}") for i in range(2)]
        ch_hi_ready, ch_lo_ready, squared = m.sem("m_ch_hi_ready"), m.sem("m_ch_lo_ready"), m.sem("m_squared")
        folded_ready = m.sem("m_folded_ready")
        res_scaled = m.sem("m_res_scaled")
        rms_summed, conv_ready, attn_ready = m.sem("m_rms_summed"), m.sem("m_conv_ready"), m.sem("m_attn_ready")
        rms_root, rms_ready = m.sem("m_rms_root"), m.sem("m_rms_ready")
        conv_added, attn_added = m.sem("m_conv_added"), m.sem("m_attn_added")
        half_stats, stats_seen, moments_ready = m.sem("m_half_stats"), m.sem("m_stats_seen"), m.sem("m_moments_ready")
        std_ready, rstd_ready, offset_ready = m.sem("m_std_ready"), m.sem("m_rstd_ready"), m.sem("m_offset_ready")
        scaled, gained, h1_ready = m.sem("m_scaled"), m.sem("m_gained"), m.sem("m_h1_ready")
        transposed, tr_copied = m.sem("m_transposed"), m.sem("m_tr_copied")
        logits_summed, logits_copied = m.sem("m_logits_summed"), m.sem("m_logits_copied")
        passed = m.sem("m_passed")
        half = KC // 2

        with nc.Block() as block:

            @block.sync
            def _(sp):
                for b in range(2):
                    sp.sem_inc(h1_sent[b], 16)
                sp.dma_start(row_gain[:], g_mix).then_inc(row_gain_landed, 16)

                def at(t):
                    return t * P if isinstance(t, int) else sp.snap(t * P)

                def load_channels(t, b, use):
                    tokens = at(t)
                    sp.wait_ge(ch_lo_ready, t + 1)
                    sp.wait_ge(squared, t + 1)
                    sp.dma_start(ch_raw[b][:], mixed_dram[:, bass.ds(tokens, P)].rearrange("(k p) t -> p k t", p=P)
                                 ).then_inc(ch_landed[b], 16)

                def load_residual(t, b, use):
                    tokens = at(t)
                    sp.wait_ge(h1_sent[b], 16 * use + 16)
                    sp.wait_ge(transposed, t + 1)
                    sp.dma_start(rows[b][:], h_dram[bass.ds(tokens, P), :]).then_inc(h_landed[b], 16)

                def send(t, b, use):
                    tokens = at(t)
                    sp.wait_ge(h1_ready, t + 1)
                    sp.dma_start(h1_dram[bass.ds(tokens, P), :], rows[b][:]).then_inc(h1_sent[b], 16)

                skewed(sp, (0, load_channels), (1, load_residual), (2, send))
                for b in range(2):
                    sp.wait_ge(h1_sent[b], 16 * (TILES // 2 + 1))

            @block.gpsimd
            def _(pool):
                pool.memset(ones[:], 1.0).then_inc(const_ready, 1)
                pool.memset(eps[:, 0:1], RMS_EPS).then_inc(const_ready, 1)
                pool.memset(eps[:, 1:2], LN_EPS).then_inc(const_ready, 1)
                pool.wait_ge(params_landed, 48)

                def add_shift(t, b, use):
                    pool.wait_ge(gained, t + 1)
                    pool.tensor_tensor(rows[b][:], rows[b][:], shift[:], ALU.add).then_inc(h1_ready, 1)

                skewed(pool, (1, add_shift))

            @block.scalar
            def _(act):
                act.dma_start(router[:], router_w.rearrange("(k p) e -> p k e", p=P)).then_inc(params_landed, 16)
                load_row(act, gain[:], ln_g, params_landed)
                load_row(act, shift[:], ln_b, params_landed)
                act.preload_act_table_set("sqrt_and_others")
                act.wait_ge(const_ready, 3)
                for k in range(KC):
                    act.wait_ge(w_gained, k + 1)
                    act.copy(w_hi[:, k, :], w_raw[:, k, :]).then_inc(w_hi_ready, 1)

                act.sem_inc(squared, 2)
                act.sem_inc(rms_root, 1)
                act.sem_inc(tr_copied, 1)
                act.sem_inc(logits_copied, 1)

                def split(t, b, use):
                    act.wait_ge(ch_landed[b], 16 * use + 16)
                    act.wait_ge(attn_ready, t + 1)
                    act.activation(square[b][:], ch_raw[b][:], ACT.Square).then_inc(squared, 1)
                    act.copy(ch_hi[b][:], ch_raw[b][:]).then_inc(ch_hi_ready, 1)

                def scale_residual(t, b, use):
                    act.wait_ge(h_landed[b], 16 * use + 16)
                    act.mul(rows[b][:], rows[b][:], ALPHA).then_inc(res_scaled, 1)

                def normalise(t, b, use):
                    act.wait_ge(rms_summed, t + 1)
                    act.wait_ge(attn_added, t + 1)
                    act.activation(rms[:], rms_ps[:, 0:2], ACT.Sqrt, scale=1.0 / D_CONV, bias=eps[:, 0:1]
                                   ).then_inc(rms_root, 1)
                    act.wait_ge(moments_ready, t + 1)
                    act.activation(rstd[:], moments[:, 1:2], ACT.Sqrt, bias=eps[:, 1:2]).then_inc(std_ready, 1)
                    act.wait_ge(offset_ready, t + 1)
                    act.activation(rows[b][:], rows[b][:], ACT.Identity, scale=rstd[:], bias=offset[:]
                                   ).then_inc(scaled, 1)

                def copy_transpose(t, b, use):
                    act.wait_ge(transposed, t + 3)
                    act.wait_ge(logits_summed, t + 1)
                    act.copy(h1_tr[:], tr_ps[:]).then_inc(tr_copied, 1)

                def copy_logits(t, b, use):
                    act.wait_ge(logits_summed, t + 2)
                    act.copy(logits[:, bass.ds(t, 1), :].rearrange("p t e -> p (t e)"), logit_ps[:, 0:EXPERTS]
                             ).then_inc(logits_copied, 1)

                skewed(act, (0, split), (1, scale_residual), (1, normalise), (2, copy_transpose), (3, copy_logits))

            @block.vector
            def _(dve):
                dve.sem_inc(ch_lo_ready, 2)
                dve.sem_inc(attn_added, 1)
                dve.sem_inc(conv_added, 1)
                dve.wait_ge(row_gain_landed, 16)
                dve.wait_ge(w_landed, 16)
                for k in range(KC):
                    dve.tensor_scalar(w_raw[:, k, :], w_raw[:, k, :], row_gain[:, k:k + 1], None, ALU.mult
                                      ).then_inc(w_gained, 1)
                    if k:
                        dve.wait_ge(w_hi_ready, k)
                        dve.tensor_tensor(w_lo[:, k - 1, :], w_raw[:, k - 1, :], w_hi[:, k - 1, :].bitcast(F32),
                                          ALU.subtract).then_inc(w_lo_ready, 1)
                dve.wait_ge(w_hi_ready, KC)
                dve.tensor_tensor(w_lo[:, KC - 1, :], w_raw[:, KC - 1, :], w_hi[:, KC - 1, :].bitcast(F32),
                                  ALU.subtract).then_inc(w_lo_ready, 1)

                def split(t, b, use):
                    dve.wait_ge(squared, t + 3)
                    dve.sem_inc(passed, 1)
                    dve.tensor_reduce(folded[b][:], square[b][:].rearrange("p (s k) t -> p s t k", s=2), AX.X, ALU.add
                                      ).then_inc(folded_ready, 1)
                    dve.wait_ge(ch_hi_ready, t + 1)
                    dve.tensor_tensor(ch_lo[b][:], ch_raw[b][:], ch_hi[b][:].bitcast(F32), ALU.subtract
                                      ).then_inc(ch_lo_ready, 1)

                def normalise(t, b, use):
                    dve.wait_ge(rms_root, t + 2)
                    dve.reciprocal(rms[:], rms[:]).then_inc(rms_ready, 1)
                    dve.wait_ge(rms_ready, t + 1)
                    dve.wait_ge(res_scaled, t + 1)
                    dve.wait_ge(conv_ready, t + 1)
                    dve.scalar_tensor_tensor(rows[b][:], conv_ps[:], rms[:, 0:1], rows[b][:], ALU.mult, ALU.add
                                             ).then_inc(conv_added, 1)
                    dve.wait_ge(conv_added, t + 2)
                    dve.wait_ge(attn_ready, t + 3)
                    dve.scalar_tensor_tensor(rows[b][:], attn_ps[:], rms[:, 1:2], rows[b][:], ALU.mult, ALU.add
                                             ).then_inc(attn_added, 1)
                    dve.wait_ge(attn_added, t + 2)
                    for n in range(2):
                        dve.bn_stats(stats[:, n, :], rows[b][:, n * BANK:(n + 1) * BANK]).then_inc(half_stats, 1)
                    dve.wait_ge(half_stats, 2 * t + 2)
                    dve.sem_inc(stats_seen, 1)
                    dve.bn_aggr(moments[:], stats[:]).then_inc(moments_ready, 1)
                    dve.wait_ge(std_ready, t + 1)
                    dve.reciprocal(rstd[:], rstd[:]).then_inc(rstd_ready, 1)
                    dve.wait_ge(rstd_ready, t + 1)
                    dve.scalar_tensor_tensor(offset[:], moments[:, 0:1], -1.0, rstd[:], ALU.mult, ALU.mult
                                             ).then_inc(offset_ready, 1)
                    dve.wait_ge(scaled, t + 1)
                    dve.tensor_tensor(rows[b][:], rows[b][:], gain[:], ALU.mult).then_inc(gained, 1)

                dve.wait_ge(params_landed, 48)
                skewed(dve, (0, split), (1, normalise))

            @block.tensor
            def _(pe):
                pe.sem_inc(attn_ready, 2)
                pe.sem_inc(transposed, 2)
                pe.sem_inc(logits_summed, 1)
                pe.wait_ge(const_ready, 3)
                pe.wait_ge(params_landed, 48)

                def product(out, t, b, first, bank):
                    terms = [(k, c, w) for k in range(first, first + half) for c, w in
                             ((ch_hi, w_hi), (ch_hi, w_lo), (ch_lo, w_hi))]
                    for n, (k, c, w) in enumerate(terms):
                        if isinstance(t, int) and t == 0 and bank == 0 and n % 3 == 0:
                            pe.wait_ge(w_lo_ready, k + 1)
                        mm = pe.matmul(out[:, bank * BANK:(bank + 1) * BANK], c[b][:, k, :],
                                       w[:, k, bank * BANK:(bank + 1) * BANK], start=n == 0, stop=n == len(terms) - 1)
                    return mm

                def products(t, b, use):
                    pe.wait_ge(folded_ready, t + 1)
                    pe.wait_ge(rms_root, t + 1)
                    for side in range(2):
                        mm = pe.matmul(rms_ps[:, side:side + 1], folded[b][:, side, :], ones[:], start=True, stop=True)
                    mm.then_inc(rms_summed, 1)
                    pe.wait_ge(ch_lo_ready, t + 3)
                    pe.wait_ge(conv_added, t + 1)
                    for bank in range(2):
                        mm = product(conv_ps, t, b, 0, bank)
                    mm.then_inc(conv_ready, 1)
                    pe.wait_ge(attn_added, t + 1)
                    for bank in range(2):
                        mm = product(attn_ps, t, b, half, bank)
                    mm.then_inc(attn_ready, 1)

                def transpose(t, b, use):
                    pe.wait_ge(h1_ready, t + 1)
                    pe.wait_ge(tr_copied, t + 1)
                    for k in range(KC):
                        mm = pe.transpose(tr_ps[:, k, :], rows[b][:, k * P:(k + 1) * P], ident[:])
                    mm.then_inc(transposed, 1)

                def route_logits(t, b, use):
                    pe.wait_ge(tr_copied, t + 2)
                    pe.wait_ge(logits_copied, t + 1)
                    for k in range(KC):
                        mm = pe.matmul(logit_ps[:, 0:EXPERTS], h1_tr[:, k, :], router[:, k, :], start=k == 0,
                                       stop=k == KC - 1)
                    mm.then_inc(logits_summed, 1)

                skewed(pe, (1, products), (3, route_logits), (2, transpose))


def route(nc, logits, weight, position_id, first_block, more_blocks, idle_blocks, slots, raw, raw_landed, router_b,
          first_weights):
    with ExitStack() as ctx:
        m = Memory(nc, ctx)
        by_expert = [P, TILES, EXPERTS]
        n_groups = TILES * GROUPS
        score, select, bias = m.sb("r_score", by_expert), m.sb("r_select", by_expert), m.sb("r_bias", [P, EXPERTS])
        high = m.sb("r_high", [P, n_groups, 2])
        low = m.sb("r_low", [P, n_groups, 2])
        top = m.sb("r_top", [P, TILES, GROUPS])
        second = m.sb("r_second", [P, TILES, GROUPS])
        group_mask = m.sb("r_group_mask", [P, TILES, GROUPS])
        best = m.sb("r_best", [P, TILES])
        product = m.sb("r_product", by_expert)
        in_group = m.sb("r_in_group", [P, TILES, PER_GROUP])
        group_score = m.sb("r_group_score", [P, TILES, PER_GROUP])
        local = [m.sb(f"r_local{i}", [P, TILES, PER_GROUP]) for i in range(TOP_K)]
        scratch = m.sb("r_scratch", [P, TILES, PER_GROUP])
        chosen = [m.sb(f"r_chosen{i}", by_expert) for i in range(TOP_K)]
        either = m.sb("r_either", by_expert)
        rank = m.sb("r_rank", by_expert)
        before = m.sb("r_before", [P, TILES + 1, EXPERTS])
        over = m.sb("r_over", [P, EXPERTS, TILES])
        n_blocks, ends = m.sb("r_n_blocks", [P, EXPERTS]), m.sb("r_ends", [P, EXPERTS])
        falling = m.sb("r_falling", [P, GROUPS])
        falling_i = m.sb("r_falling_i", [P, GROUPS], I32)
        steps_i, steps = m.sb("r_steps_i", [P, TILES], I32), m.sb("r_steps", [P, TILES])
        ones, tri = m.sb("r_ones", [P, P]), m.sb("r_tri", [P, P])
        token_id = m.sb("r_token_id", [P, TILES], I32)
        position = [m.sb(f"r_position{k}", [P, TILES]) for k in range(TOP_K)]
        slot_id = m.sb("r_slot_id", [P, TILES], I32)
        row_of, block_of = m.sb("r_row_of", [P, TILES]), m.sb("r_block_of", [P, TILES])
        token = m.sb("r_token", [P, TILES])
        count_i, count = m.sb("r_count_i", [P, P], I32), m.sb("r_count", [P, P])
        row_hot = [m.sb(f"r_row_hot{k}", [P, TILES, P]) for k in range(TOP_K)]
        block_hot = [m.sb(f"r_block_hot{k}", [P, TILES, SLOT_BLOCKS]) for k in range(TOP_K)]
        rank_ps, count_ps = m.ps("r_rank_ps", by_expert), m.ps("r_count_ps", by_expert)
        slot_ps = m.ps("r_slot_ps", [P, BANK])

        bias_landed = m.sem("r_bias_landed")
        exp_ready = m.sem("r_exp_ready")
        chain = m.sem("r_chain")
        chosen_ready = m.sem("r_chosen_ready")
        counted = m.sem("r_counted")
        pool_const = m.sem("r_pool_const")
        hot_ready = m.sem("r_hot_ready")
        slots_summed = m.sem("r_slots_summed")

        with nc.Block() as block:

            @block.sync
            def _(sp):
                load_row(sp, bias[:], router_b, bias_landed)
                for w in range(3):
                    sp.dma_start(raw[w][:], first_weights[w].rearrange("(k p) n -> p k n", p=P)
                                 ).then_inc(raw_landed[w], 16)

            @block.scalar
            def _(act):
                act.activation(score[:], logits[:], ACT.Exp, scale=-1.0).then_inc(exp_ready, 1)

            @block.gpsimd
            def _(pool):
                pool.iota(falling_i[:], [[-1, GROUPS]], base=GROUPS, channel_multiplier=0).then_inc(pool_const, 1)
                pool.iota(steps_i[:], [[P, TILES]], base=0, channel_multiplier=0).then_inc(pool_const, 1)
                pool.iota(token_id[:], [[P, TILES]], base=0, channel_multiplier=1).then_inc(pool_const, 1)
                pool.memset(ones[:], 1.0).then_inc(pool_const, 1)
                pool.iota(count_i[:], [[1, P]], base=0, channel_multiplier=0).then_inc(pool_const, 1)
                pool.memset(tri[:], 1.0).then_inc(pool_const, 1)
                pool.wait_ge(pool_const, 6)
                pool.affine_select(out=tri[:], in_=tri[:], compare_op=ALU.is_gt, fill=0.0, base=0,
                                   pattern=[[1, P]], channel_multiplier=-1).then_inc(pool_const, 1)
                pool.memset(slots[:, SLOT_BLOCKS:], 0).then_inc(pool_const, 1)

            @block.tensor
            def _(pe):
                pe.wait_ge(pool_const, 7)
                pe.wait_ge(chosen_ready, 1)
                pe.matmul(rank_ps[:], tri[:], either[:], start=True, stop=True)
                pe.matmul(count_ps[:], ones[:], either[:], start=True, stop=True).then_inc(counted, 1)
                for k in range(TOP_K):
                    pe.wait_ge(hot_ready, k + 1)
                    for t in range(TILES):
                        mm = pe.matmul(slot_ps[:, 0:SLOT_BLOCKS], row_hot[k][:, t, :], block_hot[k][:, t, :],
                                       start=k == 0 and t == 0, stop=k == TOP_K - 1 and t == TILES - 1)
                mm.then_inc(slots_summed, 1)

            @block.vector
            def _(dve):
                made = [0]

                def step(instruction):
                    made[0] += 1
                    instruction.then_inc(chain, 1)
                    dve.wait_ge(chain, made[0])

                def first_best(out, values, width):
                    shape = [P, TILES, width]
                    step(dve.tensor_reduce(best[:], values[:], AX.X, ALU.max))
                    step(dve.tensor_tensor(out[:], values[:], best[:].unsqueeze(2).to_broadcast(shape), ALU.is_ge))
                    step(dve.tensor_tensor(out[:], out[:], falling[:, GROUPS - width:].unsqueeze(1).to_broadcast(shape),
                                           ALU.mult))
                    step(dve.tensor_reduce(best[:], out[:], AX.X, ALU.max))
                    step(dve.tensor_tensor(out[:], out[:], best[:].unsqueeze(2).to_broadcast(shape), ALU.is_equal))

                dve.wait_ge(exp_ready, 1)
                step(dve.tensor_scalar(score[:], score[:], 1.0, None, ALU.add))
                step(dve.reciprocal(score[:], score[:]))
                dve.wait_ge(bias_landed, 16)
                step(dve.tensor_tensor(select[:], score[:], bias[:].unsqueeze(1).to_broadcast(by_expert), ALU.add))
                dve.wait_ge(pool_const, 7)
                step(dve.tensor_copy(falling[:], falling_i[:]))
                step(dve.tensor_copy(steps[:], steps_i[:]))
                step(dve.tensor_copy(token[:], token_id[:]))
                step(dve.tensor_copy(count[:], count_i[:]))
                four = select[:].rearrange("p t (g a b) -> p (t g) a b", a=2, b=2)
                step(dve.tensor_tensor(high[:], four[:, :, :, 0], four[:, :, :, 1], ALU.max))
                step(dve.tensor_tensor(low[:], four[:, :, :, 0], four[:, :, :, 1], ALU.min))
                flat = [x[:].rearrange("p t g -> p (t g)") for x in (top, second)]
                step(dve.tensor_tensor(flat[0], high[:, :, 0], high[:, :, 1], ALU.max))
                step(dve.tensor_tensor(flat[1], high[:, :, 0], high[:, :, 1], ALU.min))
                step(dve.tensor_tensor(low[:, :, 0], low[:, :, 0], low[:, :, 1], ALU.max))
                step(dve.tensor_tensor(flat[1], flat[1], low[:, :, 0], ALU.max))
                step(dve.tensor_tensor(top[:], top[:], second[:], ALU.add))
                first_best(group_mask, top, GROUPS)
                by_group = [P, TILES, GROUPS, PER_GROUP]
                mask4 = group_mask[:].unsqueeze(3).to_broadcast(by_group)
                for out, values in ((in_group, select), (group_score, score)):
                    split = values[:].rearrange("p t (g k) -> p t g k", k=PER_GROUP)
                    step(dve.tensor_tensor(product[:].rearrange("p t (g k) -> p t g k", k=PER_GROUP), split, mask4,
                                           ALU.mult))
                    step(dve.tensor_reduce(out[:], product[:].rearrange("p t (g k) -> p t k g", k=PER_GROUP), AX.X,
                                           ALU.add))
                first_best(local[0], in_group, PER_GROUP)
                step(dve.scalar_tensor_tensor(in_group[:], local[0][:], -3.0e38, in_group[:], ALU.mult, ALU.add))
                first_best(local[1], in_group, PER_GROUP)
                for k in range(TOP_K):
                    step(dve.tensor_tensor(scratch[:], group_score[:], local[k][:], ALU.mult))
                    step(dve.tensor_reduce(weight[k][:], scratch[:], AX.X, ALU.add))
                    step(dve.tensor_tensor(
                        chosen[k][:].rearrange("p t (g k) -> p t g k", k=PER_GROUP), mask4,
                        local[k][:].unsqueeze(2).to_broadcast(by_group), ALU.mult))
                step(dve.tensor_tensor(either[:], chosen[0][:], chosen[1][:], ALU.add))
                dve.sem_inc(chosen_ready, 1)
                step(dve.tensor_tensor(best[:], weight[0][:], weight[1][:], ALU.add))
                step(dve.reciprocal(best[:], best[:]))
                for k in range(TOP_K):
                    step(dve.tensor_tensor(weight[k][:], weight[k][:], best[:], ALU.mult))
                step(dve.memset(before[:, 0, :], 0.0))
                dve.wait_ge(counted, 1)
                for t in range(TILES):
                    step(dve.tensor_tensor(before[:, t + 1, :], count_ps[:, t, :], before[:, t, :], ALU.add))
                shape = [P, EXPERTS, TILES]
                step(dve.tensor_tensor(over[:], before[:, TILES, :].unsqueeze(2).to_broadcast(shape),
                                       steps[:].unsqueeze(1).to_broadcast(shape), ALU.is_gt))
                step(dve.tensor_reduce(n_blocks[:], over[:], AX.X, ALU.add))
                step(dve.tensor_scalar(n_blocks[:], n_blocks[:], 1.0, None, ALU.max))
                step(dve.tensor_tensor_scan(ends[:], ones[:, 0:EXPERTS], n_blocks[:], 0.0, ALU.mult, ALU.add))
                step(dve.tensor_scalar(idle_blocks[:], ends[0:1, EXPERTS - 1:EXPERTS], -1.0, float(SLOT_BLOCKS),
                                       ALU.mult, ALU.add))
                step(dve.tensor_tensor(ends[:], ends[:], n_blocks[:], ALU.subtract))
                step(dve.tensor_scalar(more_blocks[:], n_blocks[0:1, :], -1.0, None, ALU.add))
                step(dve.tensor_copy(first_block[:], ends[0:1, :]))
                step(dve.tensor_scalar(ends[:], ends[:], float(P), None, ALU.mult))
                step(dve.tensor_tensor(rank[:], rank_ps[:], before[:, 0:TILES, :], ALU.add))
                step(dve.tensor_tensor(rank[:], rank[:], ends[:].unsqueeze(1).to_broadcast(by_expert), ALU.add))
                for k in range(TOP_K):
                    step(dve.tensor_tensor(product[:], rank[:], chosen[k][:], ALU.mult))
                    step(dve.tensor_reduce(position[k][:], product[:], AX.X, ALU.add))
                    step(dve.tensor_copy(position_id[k][:], position[k][:]))
                    for part_of, operand, operation in (
                            (row_of, P - 1, ALU.bitwise_and),
                            (block_of, P.bit_length() - 1, ALU.logical_shift_right)):
                        step(dve.tensor_scalar(slot_id[:], position_id[k][:], operand, None, operation))
                        step(dve.tensor_copy(part_of[:], slot_id[:]))
                    rows, blocks = [P, TILES, P], [P, TILES, SLOT_BLOCKS]
                    step(dve.tensor_tensor(row_hot[k][:], count[:].unsqueeze(1).to_broadcast(rows),
                                           row_of[:].unsqueeze(2).to_broadcast(rows), ALU.is_equal))
                    step(dve.tensor_tensor(block_hot[k][:], count[:, 0:SLOT_BLOCKS].unsqueeze(1).to_broadcast(blocks),
                                           block_of[:].unsqueeze(2).to_broadcast(blocks), ALU.is_equal))
                    step(dve.tensor_tensor(block_hot[k][:], block_hot[k][:],
                                           token[:].unsqueeze(2).to_broadcast(blocks), ALU.mult))
                    dve.sem_inc(hot_ready, 1)
                dve.wait_ge(slots_summed, 1)
                step(dve.tensor_copy(slots[:, 0:SLOT_BLOCKS], slot_ps[:, 0:SLOT_BLOCKS]))


def experts(nc, const, raw, raw_landed, first_block, more_blocks, idle_blocks, slots, w_gate, w_up, w_down, h1_dram,
            y_dram):
    ident = const["ident"]
    half_cols = D_EXPERT // 2
    with ExitStack() as ctx:
        m = Memory(nc, ctx)
        hi = [m.sb(f"e_w_hi{w}", raw[w].shape, F32R) for w in range(3)]
        lo = [m.sb(f"e_w_lo{w}", raw[w].shape, F32R) for w in range(3)]
        block_slots = m.sb("e_block_slots", [P, 1], I32)
        tokens = m.sb("e_tokens", [P, D])
        tok_tr = [m.sb(f"e_tok_tr{i}", [P, KC, P], F32R) for i in range(2)]
        gated = m.sb("e_gated", [P, D_EXPERT])
        hidden = m.sb("e_hidden", [P, D_EXPERT])
        hid_tr = [m.sb(f"e_hid_tr{i}", [P, FC, P], F32R) for i in range(2)]
        result, zero = m.sb("e_result", [P, D]), m.sb("e_zero", [P, D])
        tok_ps = m.ps("e_tok_ps", [P, KC, P])
        gate_ps = m.ps("e_gate_ps", [P, D_EXPERT])
        half_ps = [m.ps(f"e_half_ps{i}", [P, 2, half_cols]) for i in range(2)]
        up_ps = [half_ps[i][:, 0, :] for i in range(2)]
        hid_ps = [half_ps[i][:, 1, :].rearrange("p (f t) -> p f t", t=P) for i in range(2)]
        out_ps = m.ps("e_out_ps", [P, D])

        hi_ready = [m.sem(f"e_hi_ready{w}") for w in range(3)]
        lo_ready = [m.sem(f"e_lo_ready{w}") for w in range(3)]
        picked, gathered = m.sem("e_picked"), m.sem("e_gathered")
        tok_turned, tok_hi_ready, tok_ready = m.sem("e_tok_turned"), m.sem("e_tok_hi_ready"), m.sem("e_tok_ready")
        gate_made, up_made = m.sem("e_gate_made"), m.sem("e_up_made")
        gated_ready, hidden_ready = m.sem("e_gated_ready"), m.sem("e_hidden_ready")
        hid_turned, hid_hi_ready, hid_ready = m.sem("e_hid_turned"), m.sem("e_hid_hi_ready"), m.sem("e_hid_ready")
        down_made, result_ready, result_sent = m.sem("e_down_made"), m.sem("e_result_ready"), m.sem("e_result_sent")
        zero_ready, y_cleared = m.sem("e_zero_ready"), m.sem("e_y_cleared")
        passed = [m.sem(f"e_passed{i}") for i in range(3)]
        gate, up, down = range(3)

        def part(tile, h):
            pieces = tile.shape[1] // 2
            return tile[:, h * pieces:(h + 1) * pieces, :]

        def in_order(engine, slot):
            def bounds(expert):
                start = engine.value_load(first_block[0:1, bass.ds(expert, 1)], min_val=0, max_val=SLOT_BLOCKS - 1)
                return start, engine.value_load(more_blocks[0:1, bass.ds(expert, 1)], min_val=0, max_val=TILES - 1)

            def within(block):
                return nc.s_assert_within(block, 0, SLOT_BLOCKS - 2, skip_runtime_bounds_check_because=
                                          "2 SEQ choices in blocks of 128 and a block for each idle expert "
                                          "are 63 blocks at most")

            with engine.Fori(0, EXPERTS - 1) as expert:
                start, more = bounds(expert)
                with engine.If(more > 0):
                    with engine.Fori(0, more) as k:
                        slot(within(start + k), expert, None)
                slot(within(start + more), expert, expert + 1)
            start, more = bounds(EXPERTS - 1)
            with engine.Fori(0, more + 1) as k:
                slot(within(start + k), EXPERTS - 1, None)
            return start + more + 1

        with nc.Block() as block:

            @block.sync
            def _(sp):
                with sp.Fori(0, EXPERTS - 1) as e:
                    at = sp.snap(e + 1)
                    for w, source in enumerate((w_gate, w_up, w_down)):
                        sp.wait_ge(lo_ready[w], 2 * e + 2)
                        sp.dma_start(raw[w][:], source[bass.ds(at, 1), :, :].rearrange("e (k p) n -> p (e k) n", p=P)
                                     ).then_inc(raw_landed[w], 16)
                idle = sp.value_load(idle_blocks[0:1, 0:1], min_val=1, max_val=SLOT_BLOCKS - EXPERTS)
                sp.wait_ge(zero_ready, 1)
                with sp.Fori(0, idle) as k:
                    sp.dma_start(y_dram[bass.ds(sp.snap((SLOT_BLOCKS - 1 - k) * P), P), :], zero[:]
                                 ).then_inc(y_cleared, 16)
                sp.wait_ge(y_cleared, 16 * idle)
                sp.sem_inc(passed[2], 1)

            @block.gpsimd
            def _(pool):
                def gather(block):
                    pool.tensor_copy(block_slots[:], slots[:, bass.ds(block, 1)]).then_inc(picked, 1)
                    pool.wait_ge(picked, block + 1)
                    pool.sem_inc(passed[0], 1)
                    pool.indirect_dma_start(out=tokens[:], out_offset=None, in_=h1_dram,
                                            in_offset=bass.IndirectOffsetOnAxis(ap=block_slots[:, 0:1], axis=0)
                                            ).then_inc(gathered, 16)

                def split_down(expert):
                    for h in range(2):
                        pool.wait_ge(hi_ready[down], 2 * expert + h + 1)
                        pool.tensor_tensor(part(lo[down], h), part(raw[down], h), part(hi[down], h).bitcast(F32),
                                           ALU.subtract).then_inc(lo_ready[down], 1)

                gather(0)
                pool.wait_ge(tok_turned, 1)
                gather(1)
                split_down(0)

                def slot(block, expert, following):
                    pool.wait_ge(tok_turned, block + 2)
                    pool.sem_inc(passed[0], 1)
                    gather(block + 2)
                    if following is not None:
                        split_down(following)

                blocks = in_order(pool, slot)
                pool.wait_ge(gathered, 16 * blocks + 32)
                pool.sem_inc(passed[0], 1)

            @block.scalar
            def _(act):
                act.sem_inc(result_sent, 16)

                def high(w, expert):
                    act.wait_ge(raw_landed[w], 16 * expert + 16)
                    for h in range(2):
                        act.copy(part(hi[w], h), part(raw[w], h)).then_inc(hi_ready[w], 1)

                def high_tokens(block):
                    act.wait_ge(tok_turned, block + 1)
                    act.copy(tok_tr[0][:], tok_ps[:]).then_inc(tok_hi_ready, 1)

                high(gate, 0)
                high_tokens(0)
                high(up, 0)
                high(down, 0)

                def slot(block, expert, following):
                    act.wait_ge(gate_made, block + 1)
                    act.activation(gated[:], gate_ps[:], ACT.Silu).then_inc(gated_ready, 1)
                    if following is not None:
                        high(gate, following)
                    for h in range(2):
                        act.wait_ge(hid_turned, 2 * block + h + 1)
                        act.copy(part(hid_tr[0], h), hid_ps[h]).then_inc(hid_hi_ready, 1)
                    high_tokens(block + 1)
                    if following is not None:
                        high(up, following)
                    act.wait_ge(down_made, block + 1)
                    act.wait_ge(result_sent, 16 * block + 16)
                    act.copy(result[:], out_ps[:]).then_inc(result_ready, 1)
                    if following is not None:
                        high(down, following)
                    row = act.snap(block * P)
                    act.wait_ge(result_ready, block + 2)
                    act.dma_start(y_dram[bass.ds(row, P), :], result[:]).then_inc(result_sent, 16)

                blocks = in_order(act, slot)
                act.wait_ge(result_sent, 16 * blocks + 16)
                act.sem_inc(passed[1], 1)

            @block.vector
            def _(dve):
                def low(w, expert, h):
                    dve.wait_ge(hi_ready[w], 2 * expert + h + 1)
                    dve.tensor_tensor(part(lo[w], h), part(raw[w], h), part(hi[w], h).bitcast(F32), ALU.subtract
                                      ).then_inc(lo_ready[w], 1)

                def low_tokens(block):
                    dve.wait_ge(tok_hi_ready, block + 1)
                    dve.tensor_tensor(tok_tr[1][:], tok_ps[:], tok_tr[0][:].bitcast(F32), ALU.subtract
                                      ).then_inc(tok_ready, 1)

                dve.memset(zero[:], 0.0).then_inc(zero_ready, 1)
                low(gate, 0, 0)
                low(gate, 0, 1)
                low_tokens(0)
                low(up, 0, 0)
                low(up, 0, 1)

                def slot(block, expert, following):
                    if following is not None:
                        low(gate, following, 0)
                    dve.wait_ge(gated_ready, block + 1)
                    for h in range(2):
                        cols = slice(h * half_cols, (h + 1) * half_cols)
                        dve.wait_ge(up_made, 2 * block + h + 1)
                        dve.tensor_tensor(hidden[:, cols], up_ps[h], gated[:, cols], ALU.mult
                                          ).then_inc(hidden_ready, 1)
                    for h in range(2):
                        dve.wait_ge(hid_hi_ready, 2 * block + h + 1)
                        dve.tensor_tensor(part(hid_tr[1], h), hid_ps[h], part(hid_tr[0], h).bitcast(F32),
                                          ALU.subtract).then_inc(hid_ready, 1)
                    low_tokens(block + 1)
                    if following is not None:
                        low(gate, following, 1)
                        low(up, following, 0)
                        low(up, following, 1)

                in_order(dve, slot)

            @block.tensor
            def _(pe):
                pe.sem_inc(result_ready, 1)

                def turn_tokens(block):
                    pe.wait_ge(gathered, 16 * block + 16)
                    for k in range(KC):
                        mm = pe.transpose(tok_ps[:, k, :], tokens[:, k * P:(k + 1) * P], ident[:])
                    mm.then_inc(tok_turned, 1)

                def product(out, stationary, w, expert, pieces, h, cols):
                    pe.wait_ge(lo_ready[w], 2 * expert + h + 1)
                    for k in range(h * pieces // 2, (h + 1) * pieces // 2):
                        for a, b in ((0, hi), (0, lo), (1, hi)):
                            mm = pe.matmul(out, stationary[a][:, k, :], b[w][:, k, cols],
                                           start=k == 0 and a == 0 and b is hi, stop=k == pieces - 1 and a == 1)
                    return mm

                turn_tokens(0)

                def slot(block, expert, following):
                    pe.wait_ge(tok_ready, block + 1)
                    for h in range(2):
                        mm = product(gate_ps[:], tok_tr, gate, expert, KC, h, slice(0, D_EXPERT))
                    mm.then_inc(gate_made, 1)
                    for c in range(2):
                        cols = slice(c * half_cols, (c + 1) * half_cols)
                        for h in range(2):
                            mm = product(up_ps[c], tok_tr, up, expert, KC, h, cols)
                        mm.then_inc(up_made, 1)
                    for c in range(2):
                        pe.wait_ge(hidden_ready, 2 * block + c + 1)
                        for f in range(FC // 2):
                            columns = slice(c * half_cols + f * P, c * half_cols + (f + 1) * P)
                            mm = pe.transpose(hid_ps[c][:, f, :], hidden[:, columns], ident[:])
                        mm.then_inc(hid_turned, 1)
                        if c == 0:
                            turn_tokens(block + 1)
                    pe.wait_ge(result_ready, block + 1)
                    for h in range(2):
                        pe.wait_ge(hid_ready, 2 * block + h + 1)
                        for bank in range(2):
                            cols = slice(bank * BANK, (bank + 1) * BANK)
                            mm = product(out_ps[:, cols], hid_tr, down, expert, FC, h, cols)
                    mm.then_inc(down_made, 1)

                in_order(pe, slot)


def combine(nc, weight, position_id, ln_g, ln_b, h1_dram, y_dram, out):
    ring = 4
    with ExitStack() as ctx:
        m = Memory(nc, ctx)
        gain, shift = m.sb("c_gain", [P, D]), m.sb("c_shift", [P, D])
        eps = m.sb("c_eps", [P, 1])
        rows = m.sb("c_rows", [P, TILES, D])
        picked_id = [[m.sb(f"c_picked_id{i}_{k}", [P, 1], I32) for k in range(TOP_K)] for i in range(ring)]
        y = [[m.sb(f"c_y{i}_{k}", [P, D]) for k in range(TOP_K)] for i in range(ring)]
        stats = [m.sb(f"c_stats{i}", [P, 2, 6]) for i in range(ring)]
        moments = [m.sb(f"c_moments{i}", [P, 2]) for i in range(ring)]
        rstd = [m.sb(f"c_rstd{i}", [P, 1]) for i in range(ring)]
        offset = [m.sb(f"c_offset{i}", [P, 1]) for i in range(ring)]

        params_landed = m.sem("c_params_landed")
        const_ready = m.sem("c_const_ready")
        h_landed = [m.sem(f"c_h_landed{i}") for i in range(ring)]
        y_landed = [m.sem(f"c_y_landed{i}") for i in range(ring)]
        out_sent = m.sem("c_out_sent")
        picked = m.sem("c_picked")
        passed = [m.sem(f"c_passed{i}") for i in range(3)]
        res_scaled, y_added = m.sem("c_res_scaled"), m.sem("c_y_added")
        half_stats, moments_ready = m.sem("c_half_stats"), m.sem("c_moments_ready")
        std_ready, rstd_ready, offset_ready = m.sem("c_std_ready"), m.sem("c_rstd_ready"), m.sem("c_offset_ready")
        scaled, gained, shifted = m.sem("c_scaled"), m.sem("c_gained"), m.sem("c_shifted")
        with nc.Block() as block:

            @block.sync
            def _(sp):
                load_row(sp, gain[:], ln_g, params_landed)
                load_row(sp, shift[:], ln_b, params_landed)
                with sp.Fori(0, TILES) as t:
                    sp.wait_ge(shifted, t + 1)
                    sp.dma_start(out[bass.ts(t, P), :], rows[:, t, :]).then_inc(out_sent, 16)
                sp.wait_ge(out_sent, 16 * TILES)

            @block.gpsimd
            def _(pool):
                pool.memset(eps[:], LN_EPS).then_inc(const_ready, 1)

                def gather(t, b, use):
                    pool.wait_ge(y_added, TOP_K * t + TOP_K)
                    pool.sem_inc(picked, 1)
                    for k in range(TOP_K):
                        pool.tensor_copy(picked_id[b][k][:], position_id[k][:, bass.ds(t, 1)]).then_inc(picked, 1)
                    pool.wait_ge(picked, 3 * t + 3)
                    pool.sem_inc(passed[0], 1)
                    for k in range(TOP_K):
                        pool.indirect_dma_start(out=y[b][k][:], out_offset=None, in_=y_dram,
                                                in_offset=bass.IndirectOffsetOnAxis(ap=picked_id[b][k][:, 0:1], axis=0)
                                                ).then_inc(y_landed[b], 16)

                def add_shift(t, b, use):
                    pool.wait_ge(gained, t + 1)
                    pool.tensor_tensor(rows[:, t, :], rows[:, t, :], shift[:], ALU.add).then_inc(shifted, 1)

                skewed(pool, (0, gather), (4, add_shift), ring=ring)

            @block.scalar
            def _(act):
                act.preload_act_table_set("sqrt_and_others")
                act.wait_ge(const_ready, 1)

                def load(t, b, use):
                    tokens = t * P if isinstance(t, int) else act.snap(t * P)
                    act.dma_start(rows[:, t, :], h1_dram[bass.ds(tokens, P), :]).then_inc(h_landed[b], 16)

                def scale_residual(t, b, use):
                    act.wait_ge(h_landed[b], 16 * use + 16)
                    act.sem_inc(passed[1], 1)
                    act.mul(rows[:, t, :], rows[:, t, :], ALPHA).then_inc(res_scaled, 1)

                def square_root(t, b, use):
                    act.wait_ge(moments_ready, t + 1)
                    act.activation(rstd[b][:], moments[b][:, 1:2], ACT.Sqrt, bias=eps[:]).then_inc(std_ready, 1)

                def normalise(t, b, use):
                    act.wait_ge(offset_ready, t + 1)
                    act.sem_inc(passed[2], 1)
                    act.activation(rows[:, t, :], rows[:, t, :], ACT.Identity, scale=rstd[b][:], bias=offset[b][:]
                                   ).then_inc(scaled, 1)

                skewed(act, (ring, scale_residual), (0, load), (ring + 2, normalise), (ring + 1, square_root),
                       ring=ring)

            @block.vector
            def _(dve):
                dve.sem_inc(y_added, ring * TOP_K)
                dve.wait_ge(params_landed, 32)

                def add(t, b, use):
                    dve.wait_ge(res_scaled, t + 1)
                    dve.wait_ge(y_landed[b], 32 * use + 32)
                    for k in range(TOP_K):
                        dve.scalar_tensor_tensor(rows[:, t, :], y[b][k][:], weight[k][:, bass.ds(t, 1)], rows[:, t, :],
                                                 ALU.mult, ALU.add).then_inc(y_added, 1)
                        dve.wait_ge(y_added, TOP_K * (t + ring) + k + 1)
                    dve.sem_inc(half_stats, 1)
                    for n in range(2):
                        dve.bn_stats(stats[b][:, n, :], rows[:, t, n * BANK:(n + 1) * BANK]).then_inc(half_stats, 1)

                def aggregate(t, b, use):
                    dve.wait_ge(half_stats, 4 * t + 3)
                    dve.sem_inc(half_stats, 1)
                    dve.bn_aggr(moments[b][:], stats[b][:]).then_inc(moments_ready, 1)

                def centre(t, b, use):
                    dve.wait_ge(std_ready, t + 1)
                    dve.reciprocal(rstd[b][:], rstd[b][:]).then_inc(rstd_ready, 1)
                    dve.wait_ge(rstd_ready, t + 1)
                    dve.scalar_tensor_tensor(offset[b][:], moments[b][:, 0:1], -1.0, rstd[b][:], ALU.mult, ALU.mult
                                             ).then_inc(offset_ready, 1)

                def apply_gain(t, b, use):
                    dve.wait_ge(scaled, t + 1)
                    dve.tensor_tensor(rows[:, t, :], rows[:, t, :], gain[:], ALU.mult).then_inc(gained, 1)

                skewed(dve, (0, add), (0, aggregate), (1, centre), (2, apply_gain), ring=ring)


def decoder_layer(nc, x, ln0_g, ln0_b, w_in, conv_w, g_mix, w_out, ln_mix_g, ln_mix_b, router_w, router_b,
                  w_gate, w_up, w_down, ln_ffn_g, ln_ffn_b, out):
    def scratch(name, shape, dt=F32):
        return nc.dram_tensor(name, shape, dt, kind="Internal").ap()

    h_dram, h1_dram = scratch("h_scratch", (SEQ, D)), scratch("h1_scratch", (SEQ, D))
    qk_dram = scratch("qk_scratch", (2, 2 * D_ATTN, SEQ))
    v_dram = scratch("v_scratch", (HEADS, P, TILES, 2 * HEAD_DIM))
    mixed_dram = scratch("mixed_scratch", (D, SEQ))
    y_dram = scratch("y_scratch", (SLOTS, D))
    with ExitStack() as ctx:
        m = Memory(nc, ctx)
        const = {"ident": m.sb("ident", [P, P])}
        with ExitStack() as front:
            f = Memory(nc, front)
            h_tr = [f.sb(f"h_tr{i}", [P, KC, SEQ], F32R) for i in range(2)]
            norm_input(nc, const, h_tr, x, ln0_g, ln0_b, h_dram)
            project(nc, const, h_tr, w_in, conv_w, qk_dram, v_dram, mixed_dram)
        logits = m.sb("logits", [P, TILES, EXPERTS])
        weight = [m.sb(f"weight{k}", [P, TILES]) for k in range(TOP_K)]
        position_id = [m.sb(f"position_id{k}", [P, TILES], I32) for k in range(TOP_K)]
        first_block, more_blocks = m.sb("first_block", [1, EXPERTS], I32), m.sb("more_blocks", [1, EXPERTS], I32)
        with ExitStack() as middle:
            e = Memory(nc, middle)
            w_raw, w_landed = e.sb("w_out_raw", [P, KC, D]), e.sem("w_out_landed")
            attend(nc, const, w_raw, w_landed, w_out, qk_dram, v_dram, mixed_dram)
            mix(nc, const, logits, w_raw, w_landed, g_mix, ln_mix_g, ln_mix_b, router_w, h_dram, mixed_dram, h1_dram)
        with ExitStack() as moe:
            e = Memory(nc, moe)
            shapes = ([P, KC, D_EXPERT], [P, KC, D_EXPERT], [P, FC, D])
            raw = [e.sb(f"w_raw{w}", shapes[w]) for w in range(3)]
            raw_landed = [e.sem(f"w_raw_landed{w}") for w in range(3)]
            slots = e.sb("slots", [P, SLOT_BLOCKS + 1], I32)
            idle_blocks = e.sb("idle_blocks", [1, 1], I32)
            route(nc, logits, weight, position_id, first_block, more_blocks, idle_blocks, slots, raw, raw_landed,
                  router_b, (w_gate[0], w_up[0], w_down[0]))
            experts(nc, const, raw, raw_landed, first_block, more_blocks, idle_blocks, slots, w_gate, w_up, w_down,
                    h1_dram, y_dram)
        combine(nc, weight, position_id, ln_ffn_g, ln_ffn_b, h1_dram, y_dram, out)


def kernel(x, ln0_g, ln0_b, w_in, conv_w, g_conv, g_attn, w_out, ln_mix_g, ln_mix_b, router_w, router_b,
           w_gate, w_up, w_down, ln_ffn_g, ln_ffn_b):
    import numpy as np
    import concourse.bacc as bacc
    from concourse.bass_utils import run_bass_kernel_spmd

    def plain(a):
        return np.ascontiguousarray(a)

    arrays = {
        "x": plain(x).reshape(SEQ, D), "ln0_g": plain(ln0_g), "ln0_b": plain(ln0_b),
        "w_in": plain(w_in).reshape(D, 3 * D_CONV + 3 * D_ATTN),
        "conv_w": np.ascontiguousarray(plain(conv_w).reshape(CONV_K, CC, P).transpose(2, 0, 1)),
        "g_mix": np.ascontiguousarray(np.concatenate([plain(g_conv)[0], plain(g_attn)[0]]).reshape(KC, P).T),
        "w_out": plain(w_out).reshape(D, D), "ln_mix_g": plain(ln_mix_g).reshape(D),
        "ln_mix_b": plain(ln_mix_b).reshape(D), "router_w": plain(router_w), "router_b": plain(router_b),
        "w_gate": plain(w_gate).reshape(EXPERTS, D, D_EXPERT), "w_up": plain(w_up).reshape(EXPERTS, D, D_EXPERT),
        "w_down": plain(w_down).reshape(EXPERTS, D_EXPERT, D), "ln_ffn_g": plain(ln_ffn_g).reshape(D),
        "ln_ffn_b": plain(ln_ffn_b).reshape(D),
    }
    nc = bacc.Bacc("TRN2", target_bir_lowering=False, num_devices=1)
    args = [nc.dram_tensor(f"{name}_in", a.shape, F32, kind="ExternalInput").ap() for name, a in arrays.items()]
    out = nc.dram_tensor("out", (SEQ, D), F32, kind="ExternalOutput").ap()
    decoder_layer(nc, *args, out)
    r = run_bass_kernel_spmd(nc, [{f"{name}_in": a for name, a in arrays.items()}], core_ids=[0])
    return r.results[0]["out"].reshape(1, SEQ, D)
```
